# Optimizing a Trainium2 kernel written in Bass

```python
import jax, jax.numpy as jnp
from jax import lax
import numpy as np

D_MODEL = 1024
BATCH = 1
SEQ = 2048
DEPTH = 1

CHUNK = 64
N_META = 16
Q_BLOCK = 128
D_HEAD = 64
H_A = 8
R_A = 128
H_IDX = 8
D_IDX = 64
TOPK_MAX = 256
H_B = 8
KV_B = 2
G_B = H_B // KV_B
WINDOW = 128
W_CHUNKS = WINDOW // CHUNK
H_C = 8
W_A = H_A * D_HEAD
W_B = H_B * D_HEAD
W_C = H_C * D_HEAD
D_MIX = W_A + W_B + W_C
_SIZES = (W_A, R_A, H_IDX * D_IDX, D_IDX, H_IDX, W_A,
          W_B, KV_B * D_HEAD, KV_B * D_HEAD, W_B,
          W_C, W_C, W_C, W_C)
D_IN = sum(_SIZES)
_SPLIT_AT = tuple(int(v) for v in np.cumsum(_SIZES)[:-1])
RMS_EPS = 1e-6

kernel_name = 'hybrid_dsa_swa_stickbreak_encoder'

def rmsnorm(x, g):
    xf = x.astype(jnp.float32)
    y = xf * lax.rsqrt(jnp.mean(xf * xf, axis=-1, keepdims=True) + RMS_EPS)
    return (y * g.astype(jnp.float32)).astype(x.dtype)

def alibi_slopes(n):
    return jnp.asarray([2.0 ** (-8.0 * (i + 1) / n) for i in range(n)], dtype=jnp.float32)

def chunk_id(p):
    return jnp.where(p < N_META, 0, 1 + (p - N_META) // CHUNK)

def to_blocks(a):
    b, lp = a.shape[:2]
    return jnp.moveaxis(a.reshape((b, lp // Q_BLOCK, Q_BLOCK) + a.shape[2:]), 1, 0)

def from_blocks(a):
    a = jnp.moveaxis(a, 0, 1)
    return a.reshape((a.shape[0], a.shape[1] * a.shape[2]) + a.shape[3:])

def dsa_mixer(q, ckv, q_idx, k_idx, w_idx, w_uk, w_uv, pos, k_sel):
    slopes = alibi_slopes(H_A)
    q_abs = jnp.einsum('bthd,rhd->bthr', q, w_uk)
    key_chunk = chunk_id(pos)

    def block(args):
        qa, qi, wi, qpos = args
        qchunk = chunk_id(qpos)
        rel = jax.nn.relu(jnp.einsum('bqhd,bsd->bqhs', qi, k_idx).astype(jnp.float32) * D_IDX ** -0.5)
        score = jnp.einsum('bqh,bqhs->bqs', wi.astype(jnp.float32) * H_IDX ** -0.5, rel)
        admissible = key_chunk[None, :] <= qchunk[:, None]
        score = jnp.where(admissible[None], score, -jnp.inf)
        _, idx = lax.top_k(score, k_sel)
        valid = chunk_id(idx) <= qchunk[None, :, None]
        c_sel = jax.vmap(lambda c, i: c[i])(ckv, idx)
        logits = jnp.einsum('bqhr,bqkr->bhqk', qa, c_sel).astype(jnp.float32) * D_HEAD ** -0.5
        dist = jnp.abs(qpos[None, :, None] - idx).astype(jnp.float32)
        logits = logits - slopes[None, :, None, None] * dist[:, None]
        logits = jnp.where(valid[:, None], logits, -jnp.inf)
        p = jax.nn.softmax(logits, axis=-1).astype(c_sel.dtype)
        o_lat = jnp.einsum('bhqk,bqkr->bqhr', p, c_sel)
        return jnp.einsum('bqhr,rhd->bqhd', o_lat, w_uv)

    out = lax.map(block, (to_blocks(q_abs), to_blocks(q_idx), to_blocks(w_idx), pos.reshape(-1, Q_BLOCK)))
    return from_blocks(out)

def swa_sink_mixer(q, k, v, sinks, pos):
    b, lp = q.shape[:2]
    nb = lp // Q_BLOCK
    slopes = alibi_slopes(H_B).reshape(KV_B, G_B)
    qb = q.reshape(b, nb, Q_BLOCK, KV_B, G_B, D_HEAD)

    def band(a):
        ap = jnp.pad(a, ((0, 0), (Q_BLOCK, Q_BLOCK), (0, 0), (0, 0)))
        ap = ap.reshape(b, nb + 2, Q_BLOCK, KV_B, D_HEAD)
        meta = jnp.broadcast_to(a[:, None, :N_META], (b, nb, N_META, KV_B, D_HEAD))
        return jnp.concatenate([meta, ap[:, 0:nb], ap[:, 1:nb + 1], ap[:, 2:nb + 2]], axis=2)

    kb, vb = band(k), band(v)
    qpos = pos.reshape(nb, Q_BLOCK)
    band_pos = (jnp.arange(nb, dtype=jnp.int32) * Q_BLOCK)[:, None] - Q_BLOCK + jnp.arange(3 * Q_BLOCK, dtype=jnp.int32)[None, :]
    meta_pos = jnp.broadcast_to(jnp.arange(N_META, dtype=jnp.int32)[None, :], (nb, N_META))
    kpos = jnp.concatenate([meta_pos, band_pos], axis=1)
    is_meta = jnp.concatenate([jnp.ones((nb, N_META), bool), jnp.zeros((nb, 3 * Q_BLOCK), bool)], axis=1)
    qc = chunk_id(qpos)[:, :, None]
    kc = chunk_id(kpos)[:, None, :]
    in_window = (kc <= qc) & (kc > qc - W_CHUNKS) & (kpos[:, None, :] >= N_META)
    mask = in_window | is_meta[:, None, :]
    logits = jnp.einsum('bnqkgd,bnskd->bnkgqs', qb, kb).astype(jnp.float32) * D_HEAD ** -0.5
    dist = jnp.abs(qpos[:, :, None] - kpos[:, None, :]).astype(jnp.float32)
    logits = logits - slopes[None, None, :, :, None, None] * dist[None, :, None, None]
    logits = jnp.where(mask[None, :, None, None], logits, -jnp.inf)
    sink = sinks.astype(jnp.float32).reshape(KV_B, G_B)[None, None, :, :, None, None]
    m = jnp.maximum(jnp.max(logits, axis=-1, keepdims=True), sink)
    e = jnp.exp(logits - m)
    p = e / (jnp.sum(e, axis=-1, keepdims=True) + jnp.exp(sink - m))
    o = jnp.einsum('bnkgqs,bnskd->bnqkgd', p.astype(vb.dtype), vb)
    return o.reshape(b, lp, H_B, D_HEAD)

def stick_breaking_mixer(q, k, v, pos):
    def block(args):
        qb, qpos = args
        z = jnp.einsum('bqhd,bshd->bhqs', qb, k).astype(jnp.float32) * D_HEAD ** -0.5
        causal = (pos[None, :] < qpos[:, None])[None, None]
        sp = jnp.where(causal, jax.nn.softplus(z), 0.0)
        tail = lax.cumsum(sp, axis=3, reverse=True)
        a = jnp.exp(jnp.where(causal, z - tail, -jnp.inf))
        return jnp.einsum('bhqs,bshd->bqhd', a.astype(v.dtype), v)

    out = lax.map(block, (to_blocks(q), pos.reshape(-1, Q_BLOCK)))
    return from_blocks(out)

def hybrid_layer(x, g_norm, w_in, kv_norm_g, w_uk, w_uv, sinks, w_out, pos, k_sel):
    b, lp, _ = x.shape
    h = rmsnorm(x, g_norm)
    proj = jnp.einsum('btd,de->bte', h, w_in)
    (q_a, ckv, q_i, k_i, w_i, g_a, q_b, k_b, v_b, g_b, q_c, k_c, v_c, g_c) = jnp.split(proj, _SPLIT_AT, axis=-1)
    ckv = rmsnorm(ckv, kv_norm_g)
    y_a = dsa_mixer(q_a.reshape(b, lp, H_A, D_HEAD), ckv, q_i.reshape(b, lp, H_IDX, D_IDX),
                    k_i, w_i, w_uk, w_uv, pos, k_sel)
    y_b = swa_sink_mixer(q_b.reshape(b, lp, H_B, D_HEAD), k_b.reshape(b, lp, KV_B, D_HEAD),
                         v_b.reshape(b, lp, KV_B, D_HEAD), sinks, pos)
    y_c = stick_breaking_mixer(q_c.reshape(b, lp, H_C, D_HEAD), k_c.reshape(b, lp, H_C, D_HEAD),
                               v_c.reshape(b, lp, H_C, D_HEAD), pos)
    y = jnp.concatenate([y_a.reshape(b, lp, W_A) * jax.nn.silu(g_a),
                         y_b.reshape(b, lp, W_B) * jax.nn.silu(g_b),
                         y_c.reshape(b, lp, W_C) * jax.nn.silu(g_c)], axis=-1)
    return x + jnp.einsum('bte,ed->btd', y, w_out).astype(x.dtype)

def setup_inputs(seed: int = 0) -> dict:
    key = jax.random.key(seed)
    ks = jax.random.split(key, 10)
    f32 = jnp.float32
    x = jax.random.normal(ks[0], (BATCH, SEQ, D_MODEL), f32)
    meta_tokens = jax.random.normal(ks[1], (N_META, D_MODEL), f32)
    norm_g = 1.0 + 0.1 * jax.random.normal(ks[2], (DEPTH, D_MODEL), f32)
    w_in = jax.random.normal(ks[3], (DEPTH, D_MODEL, D_IN), f32) * D_MODEL ** -0.5
    kv_norm_g = 1.0 + 0.1 * jax.random.normal(ks[4], (DEPTH, R_A), f32)
    w_uk = jax.random.normal(ks[5], (DEPTH, R_A, H_A, D_HEAD), f32) * R_A ** -0.5
    w_uv = jax.random.normal(ks[6], (DEPTH, R_A, H_A, D_HEAD), f32) * R_A ** -0.5
    sinks = 0.5 * jax.random.normal(ks[7], (DEPTH, H_B), f32)
    w_out = jax.random.normal(ks[8], (DEPTH, D_MIX, D_MODEL), f32) * D_MIX ** -0.5
    final_norm_g = 1.0 + 0.1 * jax.random.normal(ks[9], (D_MODEL,), f32)
    return {'x': x, 'meta_tokens': meta_tokens, 'norm_g': norm_g, 'w_in': w_in,
            'kv_norm_g': kv_norm_g, 'w_uk': w_uk, 'w_uv': w_uv, 'sinks': sinks,
            'w_out': w_out, 'final_norm_g': final_norm_g}

def reference(x, meta_tokens, norm_g, w_in, kv_norm_g, w_uk, w_uv, sinks, w_out, final_norm_g):
    b, seq, d = x.shape
    total = N_META + seq
    lp = -(-total // Q_BLOCK) * Q_BLOCK
    k_sel = min(TOPK_MAX, seq // 4)
    meta = jnp.broadcast_to(meta_tokens.astype(x.dtype)[None], (b, N_META, d))
    h = jnp.concatenate([meta, x, jnp.zeros((b, lp - total, d), x.dtype)], axis=1)
    pos = jnp.arange(lp, dtype=jnp.int32)
    for l in range(DEPTH):
        h = hybrid_layer(h, norm_g[l], w_in[l], kv_norm_g[l], w_uk[l], w_uv[l], sinks[l], w_out[l], pos, k_sel)
    h = rmsnorm(h, final_norm_g)
    return h[:, N_META:N_META + seq]


_drawn_inputs = setup_inputs


def setup_inputs(seed=0):
    import zlib

    import numpy as np

    out = dict(_drawn_inputs(seed))
    spreads = {}
    factors = {'meta_tokens': 4.949, 'kv_norm_g': 3.195, 'sinks': 63.389}
    for name, (base, spread) in spreads.items():
        noise = np.random.default_rng([zlib.crc32(name.encode()), seed]).standard_normal(out[name].shape)
        drawn = base * np.exp(spread * noise) if base else spread * noise
        out[name] = __import__('jax').numpy.asarray(drawn.astype(out[name].dtype))
    for name, factor in factors.items():
        out[name] = (out[name] * factor).astype(out[name].dtype)
    return out
```

```python
from contextlib import ExitStack

import concourse.bass as bass
from concourse import mybir
import numpy as np

F32 = mybir.dt.float32
F32R = mybir.dt.float32r
BF16 = mybir.dt.bfloat16
ALU = mybir.AluOpType
ACT = mybir.ActivationFunctionType
AX_X = mybir.AxisListType.X

P = 128
SEQ, D_MODEL = 2048, 1024
N_META = 16
NKEY = N_META + SEQ
BLOCKS = SEQ // P
KT = D_MODEL // P
HEADS, DH = 8, 64
KV_B = 2
TOPK = 256
EPS = 1e-6
BIG = 1e30

(C_QA, C_CKV, C_QI, C_KI, C_WI, C_GA, C_QB, C_KB, C_VB, C_GB, C_QC, C_KC, C_VC, C_GC) = (
    0, 512, 640, 1152, 1216, 1224, 1736, 2248, 2376, 2504, 3016, 3528, 4040, 4552)
D_IN = 5064

WCOLS = 264


def key_tile(t):
    return (0, N_META) if t == 0 else (N_META + P * (t - 1), P)


def block_keys(j):
    return N_META + P * (j + 1)


def projection_items():
    items = [("rows", "latent", [(C_CKV, 128), (C_WI, 8), (C_VB, 128)]),
             ("cols", "k_i", C_KI, 1, 0)]
    items += [("cols", "q_i", C_QI + 256 * i, 2, 4 * i) for i in range(2)]
    items += [("cols", "k_c", C_KC + 256 * i, 2, 4 * i) for i in range(2)]
    items += [("rows", "v_c", [(C_VC + 256 * i, 256)]) for i in range(2)]
    items += [("cols", "q_c", C_QC + 256 * i, 2, 4 * i) for i in range(2)]
    items += [("cols", "k_b", C_KB, 1, 0)]
    items += [("cols", "q_a", C_QA + 256 * i, 2, 4 * i) for i in range(2)]
    items += [("cols", "q_b", C_QB + 256 * i, 2, 4 * i) for i in range(2)]
    items += [("cols", "gate", c + 256 * i, 2, n + 2 * i)
              for n, c in ((0, C_GA), (4, C_GB), (8, C_GC)) for i in range(2)]
    return items


def projection_groups():
    groups = []
    for i, item in enumerate(projection_items()):
        if item[0] == "rows":
            for t in range(BLOCKS + 1):
                groups.append((i, "rows", item[1], t, key_tile(t)))
        else:
            _, name, _, tiles, first = item
            for m in range(tiles):
                if name[0] == "k":
                    groups.append((i, "cols", name, m, (0, N_META)))
                for c in range(4):
                    groups.append((i, "cols", name, m, (N_META + 512 * c, 512)))
    for m in range(4):
        for c in range(-1, 4):
            groups.append((-1, "k_a", "k_a", m, (0, N_META) if c < 0 else (N_META + 512 * c, 512)))
    for t in range(BLOCKS + 1):
        groups.append((-1, "v_a", "v_a", t, key_tile(t)))
    return groups


def project(nc, x, meta_tokens, norm_g, w_in, kv_norm_g, w_uk, w_uv, ident, q_scale, scr):
    items = projection_items()
    groups = projection_groups()
    width = [sum(w for _, w in it[2]) if it[0] == "rows" else 128 * it[3] for it in items]
    parts = [it[2] if it[0] == "rows" else [(it[2], 128 * it[3])] for it in items]
    first_group = {}
    last_group = {}
    for u, g in enumerate(groups):
        first_group.setdefault(g[0], u)
        last_group[g[0]] = u
    BANKS = 4
    STAGES = 3
    TILES = BLOCKS + 1
    has_low = [g[1] in ("cols", "k_a") and g[2] != "gate" for g in groups]
    lows = np.cumsum([0] + [int(b) for b in has_low]).tolist()
    latent = [u for u, g in enumerate(groups) if g[2] == "latent"]

    with ExitStack() as ctx:
        def sb(name, shape, dt=F32):
            return ctx.enter_context(nc.sbuf_tensor(name, shape, dt))

        def sem(name):
            return ctx.enter_context(nc.semaphore(name))

        ps = ctx.enter_context(nc.psum_tensor("ps", [P, 8, 512], F32))
        h_hi = sb("h_hi", [P, KT, NKEY], F32R)
        h_lo = sb("h_lo", [P, KT, NKEY], F32R)
        w_raw = sb("w_raw", [P, KT, WCOLS])
        w_hi = sb("w_hi", [P, 2, KT, WCOLS], F32R)
        w_lo = sb("w_lo", [P, 2, KT, WCOLS], F32R)
        st_hi = sb("st_hi", [P, STAGES, 512])
        st_lo = sb("st_lo", [P, STAGES, 512])
        latT = sb("latT", [P, NKEY])
        wuk = sb("wuk", [P, 512])
        wuv = sb("wuv", [P, 512])
        xt = sb("xt", [P, 2, D_MODEL])
        eye = sb("eye", [P, P])
        gT = sb("gT", [P, KT])
        kvg = sb("kvg", [P, 1])
        qs = sb("qs", [P, 4])
        norm = sb("norm", [P, 4, TILES])
        lnorm = sb("lnorm", [P, 4, TILES])
        newton = sb("newton", [P, 2])
        lat = sb("lat", [P, 2, P])
        wi = sb("wi", [P, TILES, HEADS])

        const_in = sem("const_in")
        x_in = [sem(f"x_in{i}") for i in range(2)]
        sq_done, ms_done, root_done = sem("sq_done"), sem("ms_done"), sem("root_done")
        inv_done, xn_done, xT_done = sem("inv_done"), sem("xn_done"), sem("xT_done")
        h_hi_done, h_lo_done = sem("h_hi_done"), sem("h_lo_done")
        w_in_sem = sem("w_in_sem")
        w_hi_done, w_lo_done = sem("w_hi_done"), sem("w_lo_done")
        grp_done, hi_out, lo_out = sem("grp_done"), sem("hi_out"), sem("lo_out")
        hi_st = [sem(f"hi_st{i}") for i in range(STAGES)]
        lo_st = [sem(f"lo_st{i}") for i in range(STAGES)]
        lsq_done, lms_done, lroot_done = sem("lsq_done"), sem("lms_done"), sem("lroot_done")
        linv_done, lat_done, latT_ps, latT_done = sem("linv_done"), sem("lat_done"), sem("latT_ps"), sem("latT_done")
        wi_done, wi_st = sem("wi_done"), sem("wi_st")

        block = ctx.enter_context(nc.Block())

        def stores(u):
            _, kind, name, m, (c0, n) = groups[u]
            out = []
            if name == "latent":
                out.append((scr["v_b"][c0:c0 + n, :], (slice(0, n), slice(136, 264)), 0))
            elif name == "v_c":
                i = groups[u][0] - [it[1] for it in items].index("v_c")
                out.append((scr["v_c"][c0:c0 + n, 256 * i:256 * i + 256], (slice(0, n), slice(0, 256)), 0))
            elif name == "v_a":
                out.append((scr["v_a"][c0:c0 + n, :], (slice(0, n), slice(0, 512)), 0))
            elif name == "gate":
                tile = items[groups[u][0]][4] + m
                b = (c0 - N_META) // P
                out.append((scr["gate"][b:b + 4, :, tile, :].rearrange("b p q -> p b q"),
                            (slice(0, P), slice(0, 512)), 0))
            elif name[0] == "q":
                head = items[groups[u][0]][4] + 2 * m
                b = (c0 - N_META) // P
                for part in range(2):
                    for k in range(2):
                        out.append((scr[name][b:b + 4, part, :, head + k, :].rearrange("b d q -> d b q"),
                                    (slice(64 * k, 64 * k + 64), slice(0, 512)), part))
            else:
                head = 2 * m if name == "k_a" else items[groups[u][0]][4] + 2 * m
                for part in range(2):
                    for k in range(1 if name == "k_i" else 2):
                        out.append((scr[name][part, :, head + k, c0:c0 + n],
                                    (slice(64 * k, 64 * k + 64), slice(0, n)), part))
            return out

        hi_count, lo_count, hi_val, lo_val = [0] * STAGES, [0] * STAGES, [], []
        for u in range(len(groups)):
            for _, _, part in stores(u):
                if part == 0:
                    hi_count[u % STAGES] += 16
                else:
                    lo_count[lows[u] % STAGES] += 16
            hi_val.append(hi_count[u % STAGES])
            if has_low[u]:
                lo_val.append(lo_count[lows[u] % STAGES])

        def high_scale(name, g):
            if name in ("q_a", "q_b"):
                tile = (items[g[0]][4] + 2 * g[3]) // 2
                return qs[:, tile:tile + 1]
            return DH ** -0.5 if name[0] == "q" else 1.0

        @block.sync
        def _(sp):
            for dst, src in ((eye[:], ident), (gT[:], norm_g),
                             (kvg[:], kv_norm_g), (qs[:], q_scale),
                             (wuk[:], w_uk[0].rearrange("r h d -> r (h d)")),
                             (wuv[:], w_uv[0].rearrange("r h d -> r (h d)"))):
                sp.dma_start(dst, src).then_inc(const_in, 16)

            def load_x(t):
                c0, n = key_tile(t)
                if t >= 2:
                    sp.wait_ge(xT_done, t - 1)
                src = meta_tokens if t == 0 else x[0, P * (t - 1):P * t, :]
                sp.dma_start(xt[0:n, t % 2, :], src).then_inc(x_in[t % 2], 16)

            def load_w(i):
                if i >= 1:
                    sp.wait_ge(w_hi_done, i)
                    sp.wait_ge(w_lo_done, i)
                at = 0
                for c, w in parts[i]:
                    sp.dma_start(w_raw[:, :, at:at + w],
                                 w_in[0, :, c:c + w].rearrange("(k p) n -> p k n", p=P)).then_inc(w_in_sem, 16)
                    at += w

            load_w(0)
            for t in range(TILES):
                load_x(t)
            load_w(1)
            for u, g in enumerate(groups):
                if g[0] >= 0 and u == first_group[g[0]] and 2 <= g[0] + 1 < len(items):
                    load_w(g[0] + 1)
                sp.wait_ge(hi_out, u + 1)
                if has_low[u]:
                    sp.wait_ge(lo_out, lows[u + 1])
                for dst, (rows, cols), part in stores(u):
                    if part == 0:
                        sp.dma_start(dst, st_hi[rows, u % STAGES, cols]).then_inc(hi_st[u % STAGES], 16)
                    else:
                        s = lows[u] % STAGES
                        sp.dma_start(dst, st_lo[rows, s, cols]).then_inc(lo_st[s], 16)
                if u == latent[-1]:
                    sp.wait_ge(wi_done, TILES)
                    sp.dma_start(scr["w_i"], wi[:, 1:, :]).then_inc(wi_st, 16)
            for s in range(STAGES):
                sp.wait_ge(hi_st[s], hi_count[s])
                sp.wait_ge(lo_st[s], lo_count[s])
            sp.wait_ge(wi_st, 16)

        w_dmas = np.cumsum([len(p) for p in parts]).tolist()

        @block.gpsimd
        def _(pool):
            for i in range(len(items)):
                pool.wait_ge(w_in_sem, 16 * w_dmas[i])
                pool.wait_ge(w_hi_done, i + 1)
                if i >= 2:
                    pool.wait_ge(grp_done, last_group[i - 2] + 1)
                w = width[i]
                nc.gpsimd.tensor_tensor(w_lo[:, i % 2, :, 0:w], w_raw[:, :, 0:w],
                                        w_hi[:, i % 2, :, 0:w].bitcast(F32), ALU.subtract).then_inc(w_lo_done, 1)

        @block.scalar
        def _(act):
            act.wait_ge(const_in, 96)

            def split_w(i):
                act.wait_ge(w_in_sem, 16 * w_dmas[i])
                if i >= 2:
                    act.wait_ge(grp_done, last_group[i - 2] + 1)
                nc.scalar.activation(w_hi[:, i % 2, :, 0:width[i]], w_raw[:, :, 0:width[i]],
                                     ACT.Copy).then_inc(w_hi_done, 1)

            def square(t):
                _, n = key_tile(t)
                act.wait_ge(x_in[t % 2], 16 * (t // 2 + 1))
                junk = st_hi[0:n, 0:2, :].rearrange("p a b -> p (a b)")
                nc.scalar.activation(junk, xt[0:n, t % 2, :], ACT.Square,
                                     accum_out=norm[0:n, 0, t:t + 1]).then_inc(sq_done, 1)
                act.wait_ge(ms_done, t + 1)
                nc.scalar.activation(norm[0:n, 2, t:t + 1], norm[0:n, 1, t:t + 1], ACT.Sqrt).then_inc(root_done, 1)

            def h_high(t):
                c0, n = key_tile(t)
                act.wait_ge(xT_done, t + 1)
                for k in range(KT):
                    b = 2 * (t % 2) + k // 4
                    last = nc.scalar.activation(h_hi[:, k, c0:c0 + n], ps[:, b, P * (k % 4):P * (k % 4) + n],
                                                ACT.Copy, scale=gT[:, k:k + 1])
                last.then_inc(h_hi_done, 1)

            def latent_scale(t):
                c0, n = key_tile(t)
                u = latent[t]
                src = ps[0:n, 4 + u % BANKS, :]
                nc.scalar.activation(st_lo[0:n, 0, 0:128], src[:, 0:128], ACT.Square,
                                     accum_out=lnorm[0:n, 0, t:t + 1]).then_inc(lsq_done, 1)
                nc.scalar.activation(wi[0:n, t, :], src[:, 128:136], ACT.Copy, scale=HEADS ** -0.5).then_inc(wi_done, 1)
                act.wait_ge(lms_done, t + 1)
                nc.scalar.activation(lnorm[0:n, 2, t:t + 1], lnorm[0:n, 1, t:t + 1], ACT.Sqrt).then_inc(lroot_done, 1)

            def latent_copy(t):
                c0, n = key_tile(t)
                act.wait_ge(latT_ps, t + 1)
                nc.scalar.activation(latT[:, c0:c0 + n], ps[:, t % 2, 0:n], ACT.Copy,
                                     scale=kvg[:, 0:1]).then_inc(latT_done, 1)

            split_w(0)
            for t in range(TILES + 1):
                if t < TILES:
                    square(t)
                if t >= 1:
                    h_high(t - 1)
            split_w(1)
            for u, (i, kind, name, m, (c0, n)) in enumerate(groups):
                if i >= 0 and u == first_group[i] + 3 and 2 <= i + 1 < len(items):
                    split_w(i + 1)
                act.wait_ge(grp_done, u + 1)
                if u >= STAGES:
                    act.wait_ge(hi_st[u % STAGES], hi_val[u - STAGES])
                    if groups[u - STAGES][2] == "latent":
                        act.wait_ge(lat_done, groups[u - STAGES][3] + 1)
                bank = ps[:, 4 + u % BANKS, :]
                stage = st_hi[:, u % STAGES, :]
                if name == "latent":
                    ins = nc.scalar.activation(stage[0:n, 0:264], bank[0:n, 0:264], ACT.Copy)
                elif name == "v_c":
                    ins = nc.scalar.activation(stage[0:n, 0:256], bank[0:n, 0:256], ACT.Copy)
                elif name == "v_a":
                    ins = nc.scalar.activation(stage[0:n, :], bank[0:n, :], ACT.Copy)
                elif name == "gate":
                    ins = nc.scalar.activation(stage[:, 0:n], bank[:, 0:n], ACT.Silu)
                else:
                    scale = high_scale(name, groups[u])
                    ins = nc.scalar.activation(stage[:, 0:n].bitcast(F32R), bank[:, 0:n], ACT.Copy, scale=scale)
                ins.then_inc(hi_out, 1)
                if name == "latent":
                    latent_scale(m)
                    if m >= 1:
                        latent_copy(m - 1)
                    if m == TILES - 1:
                        latent_copy(m)

        @block.vector
        def _(dve):
            dve.wait_ge(const_in, 96)

            def mean_square(t, at, count, sq, ms):
                _, n = key_tile(t)
                dve.wait_ge(sq, t + 1)
                nc.vector.tensor_scalar(at[0:n, 1, t:t + 1], at[0:n, 0, t:t + 1], 1.0 / count, EPS,
                                        ALU.mult, ALU.add).then_inc(ms, 1)

            def inverse(t, at, root, inv):
                _, n = key_tile(t)
                dve.wait_ge(root, t + 1)
                mean, y = at[0:n, 1, t:t + 1], at[0:n, 3, t:t + 1]
                steps = 4 * t
                nc.vector.reciprocal(y, at[0:n, 2, t:t + 1]).then_inc(inv, 1)
                dve.wait_ge(inv, steps + 1)
                nc.vector.tensor_scalar(newton[0:n, 0:1], y, y, mean, ALU.mult, ALU.mult).then_inc(inv, 1)
                dve.wait_ge(inv, steps + 2)
                nc.vector.tensor_scalar(newton[0:n, 1:2], newton[0:n, 0:1], -0.5, 1.5, ALU.mult, ALU.add).then_inc(inv, 1)
                dve.wait_ge(inv, steps + 3)
                nc.vector.tensor_scalar(y, y, newton[0:n, 1:2], None, ALU.mult).then_inc(inv, 1)
                dve.wait_ge(inv, steps + 4)

            def normalise(t):
                _, n = key_tile(t)
                mean_square(t, norm, D_MODEL, sq_done, ms_done)
                inverse(t, norm, root_done, inv_done)
                nc.vector.tensor_scalar(xt[0:n, t % 2, :], xt[0:n, t % 2, :], norm[0:n, 3, t:t + 1], None,
                                        ALU.mult).then_inc(xn_done, 1)

            def h_low(t):
                c0, n = key_tile(t)
                dve.wait_ge(h_hi_done, t + 1)
                for k in range(KT):
                    b = 2 * (t % 2) + k // 4
                    last = nc.vector.scalar_tensor_tensor(
                        out=h_lo[:, k, c0:c0 + n], in0=ps[:, b, P * (k % 4):P * (k % 4) + n], scalar=gT[:, k:k + 1],
                        in1=h_hi[:, k, c0:c0 + n].bitcast(F32), op0=ALU.mult, op1=ALU.subtract)
                last.then_inc(h_lo_done, 1)

            for t in range(TILES + 1):
                if t < TILES:
                    normalise(t)
                if t >= 1:
                    h_low(t - 1)
            for u, (i, kind, name, m, (c0, n)) in enumerate(groups):
                bank = ps[:, 4 + u % BANKS, :]
                if name == "latent":
                    mean_square(m, lnorm, P, lsq_done, lms_done)
                    inverse(m, lnorm, lroot_done, linv_done)
                    if m >= 2:
                        dve.wait_ge(latT_ps, m - 1)
                    nc.vector.tensor_scalar(lat[0:n, m % 2, :], st_hi[0:n, u % STAGES, 0:128], lnorm[0:n, 3, m:m + 1], None,
                                            ALU.mult).then_inc(lat_done, 1)
                if has_low[u]:
                    s = lows[u] % STAGES
                    dve.wait_ge(hi_out, u + 1)
                    if lows[u] >= STAGES:
                        dve.wait_ge(lo_st[s], lo_val[lows[u] - STAGES])
                    nc.vector.scalar_tensor_tensor(
                        out=st_lo[:, s, 0:n].bitcast(F32R), in0=bank[:, 0:n], scalar=high_scale(name, groups[u]),
                        in1=st_hi[:, u % STAGES, 0:n], op0=ALU.mult, op1=ALU.subtract).then_inc(lo_out, 1)

        @block.tensor
        def _(pe):
            pe.wait_ge(const_in, 96)
            for t in range(TILES):
                _, n = key_tile(t)
                pe.wait_ge(xn_done, t + 1)
                if t >= 2:
                    pe.wait_ge(h_hi_done, t - 1)
                    pe.wait_ge(h_lo_done, t - 1)
                for k in range(KT):
                    b = 2 * (t % 2) + k // 4
                    last = nc.tensor.transpose(ps[:, b, P * (k % 4):P * (k % 4) + n],
                                               xt[0:n, t % 2, P * k:P * k + P], eye[0:n, 0:n])
                last.then_inc(xT_done, 1)

            def latent_transpose(t):
                _, n = key_tile(t)
                pe.wait_ge(lat_done, t + 1)
                if t >= 2:
                    pe.wait_ge(latT_done, t - 1)
                nc.tensor.transpose(ps[:, t % 2, 0:n], lat[0:n, t % 2, :], eye[0:n, 0:n]).then_inc(latT_ps, 1)

            pe.wait_ge(h_hi_done, TILES)
            pe.wait_ge(h_lo_done, TILES)
            for u, (i, kind, name, m, (c0, n)) in enumerate(groups):
                bank = ps[:, 4 + u % BANKS, :]
                if i >= 0 and u == first_group[i]:
                    pe.wait_ge(w_hi_done, i + 1)
                    pe.wait_ge(w_lo_done, i + 1)
                if u >= BANKS:
                    pe.wait_ge(hi_out, u - BANKS + 1)
                    if has_low[u - BANKS]:
                        pe.wait_ge(lo_out, lows[u - BANKS + 1])
                    if groups[u - BANKS][2] == "latent":
                        pe.wait_ge(lroot_done, groups[u - BANKS][3] + 1)
                if kind in ("rows", "cols"):
                    for k in range(KT):
                        for n_pass, (wp, hp) in enumerate(((w_hi, h_hi), (w_lo, h_hi), (w_hi, h_lo))):
                            if kind == "rows":
                                out = bank[0:n, 0:width[i]]
                                still, moving = hp[:, k, c0:c0 + n], wp[:, i % 2, k, 0:width[i]]
                                if n < P:
                                    still = hp[:, k, 0:P]
                                    out = bank[:, 0:width[i]]
                            else:
                                out = bank[:, 0:n]
                                still, moving = wp[:, i % 2, k, P * m:P * m + P], hp[:, k, c0:c0 + n]
                            ins = nc.tensor.matmul(out, still, moving, start=(k == 0 and n_pass == 0),
                                                   stop=(k == KT - 1 and n_pass == 2))
                elif kind == "k_a":
                    ins = nc.tensor.matmul(bank[:, 0:n], wuk[:, P * m:P * m + P], latT[:, c0:c0 + n],
                                           start=True, stop=True)
                else:
                    ins = nc.tensor.matmul(bank[0:n, :], latT[:, c0:c0 + n], wuv[:], start=True, stop=True)
                ins.then_inc(grp_done, 1)
                if name == "latent":
                    if m >= 1:
                        latent_transpose(m - 1)
                    if m == TILES - 1:
                        latent_transpose(m)
                        pe.wait_ge(latT_done, TILES)
F16 = mybir.dt.float16
U8 = mybir.dt.uint8
LAG = 2
UNIT = 512
SLOTS = 3
T_BANKS = 3
T_BUFS = 3
MIDDLE = 0.5
AHEAD = 10
BEHIND = 2
ROUNDS = 24
HUGE = 3e38


def head_steps():
    return [(j, h) for j in range(BLOCKS) for h in range(HEADS)]


def unit_columns(j):
    n = block_keys(j)
    return [(c, min(c + UNIT, n)) for c in range(0, n, UNIT)]


def tile_groups(j):
    real = list(range(1, j + 2))
    return [real[i:i + 4] for i in range(0, len(real), 4)] + [[0]]


class Transposes:

    def __init__(self, step_tiles, closing, dve_share=0):
        self.groups, self.by_step, self.copier, self.rank, self.slot = [], [], [], [], []
        counts = {"act": 0, "dve": 0, "gate": 0}
        slots = 0
        for w in range(len(step_tiles) + 2):
            own = [(w, tiles) for tiles in (step_tiles[w] if w < len(step_tiles) else [])]
            if w - 2 in closing:
                own.append((w, ("out", closing[w - 2])))
            self.by_step.append(list(range(len(self.groups), len(self.groups) + len(own))))
            for k, g in enumerate(own):
                copier = "gate" if g[1][0] == "out" else "dve" if dve_share and k % dve_share == dve_share - 1 else "act"
                self.groups.append(g)
                self.copier.append(copier)
                self.rank.append(counts[copier])
                self.slot.append(None if copier == "gate" else slots)
                counts[copier] += 1
                slots += copier != "gate"
        self.of_slot = [g for g, n in enumerate(self.slot) if n is not None]

    def last(self, w):
        return [g for g in self.by_step[w] if self.copier[g] != "gate"][-1]


def mix(*lists):
    return [x for _, _, x in sorted(((i + 0.5) / len(a), n, x) for n, a in enumerate(lists) for i, x in enumerate(a))]


def two_pass_scores(nc, out, q_two, k_two, c0, c1):
    for a in range(c0, c1, 512):
        b = min(a + 512, c1)
        for part in range(2):
            ins = nc.tensor.matmul(out[:, a - c0:b - c0], q_two[part], k_two[:, a:b],
                                   start=(part == 0), stop=(part == 1))
    return ins


def stick_and_select(nc, ident, stick_mask, halves, scr):
    steps = head_steps()
    S = len(steps)
    units, first_unit = [], []
    for s in range(-AHEAD, S):
        j, h = divmod(s, HEADS)
        ji, hi = divmod(s + AHEAD, HEADS)
        first_unit.append(len(units))
        if j >= 0:
            units += [("stick", j, h, c0, c1) for c0, c1 in unit_columns(j)]
        if ji < BLOCKS:
            units += [("index", ji, hi, c0, c1) for c0, c1 in unit_columns(ji)]
    first_unit.append(len(units))
    after = {}
    n_index = [0]
    for u, (kind, j, h, _, _) in enumerate(units):
        after[kind, j, h] = u + 1
        n_index.append(n_index[-1] + (kind == "index"))
    tr = Transposes([tile_groups(j) for j, _ in steps], {HEADS * j + HEADS - 1: j for j in range(BLOCKS)})

    CLOSE = LAG

    with ExitStack() as ctx:
        def sb(name, shape, dt=F32):
            return ctx.enter_context(nc.sbuf_tensor("c_" + name, shape, dt))

        def sem(name):
            return ctx.enter_context(nc.semaphore("c_" + name))

        ps = ctx.enter_context(nc.psum_tensor("c_ps", [P, 8, 512], F32))
        kc = sb("kc", [P, HEADS, NKEY], F32R)
        ki = sb("ki", [P, NKEY], F32R)
        vc = sb("vc", [P, BLOCKS + 1, 512])
        vprev = sb("vprev", [P, 512])
        qc = sb("qc", [P, 2, HEADS, P], F32R)
        qi = sb("qi", [P, 2, HEADS, P], F32R)
        wi = sb("wi", [P, BLOCKS, HEADS])
        eye = sb("eye", [P, P])
        eye16 = sb("eye16", [P, P], BF16)
        mask = sb("mask", [P, P], BF16)
        relu = sb("relu", [P, SLOTS, UNIT])
        rem = sb("rem", [P, 3, NKEY])
        score = sb("score", [P, 3, NKEY])
        junk = sb("junk", [P, 2, NKEY], U8)
        above_hi = sb("above_hi", [P, NKEY], U8)
        between = sb("between", [P, NKEY], BF16)
        order = sb("order", [P, NKEY], F16)
        pT = sb("pT", [P, T_BUFS, 512])
        y = sb("y", [P, 512])
        gate = sb("gate", [P, 4, P])
        prod = sb("prod", [P, 512])
        pow2 = sb("pow2", [P, ROUNDS])
        zeros = sb("zeros", [P, 1])
        ones = sb("ones", [P, 1])
        ext = sb("ext", [P, 2, 8])
        wid = sb("wid", [P, ROUNDS])
        mids = sb("mids", [P, ROUNDS + 1])
        cnt = sb("cnt", [P, ROUNDS])
        up = sb("up", [P, ROUNDS])
        cand = sb("cand", [P, 2, ROUNDS])

        mask_done = sem("mask_done")
        const_in, ki_in, kc_in, qi_in = sem("const_in"), sem("ki_in"), [sem(f"kc_in{i}") for i in range(4)], sem("qi_in")
        qc_in, v_in, v_meta_in = [sem(f"qc_in{i}") for i in range(2)], sem("v_in"), sem("v_meta_in")
        v_zero, v_done = sem("v_zero"), sem("v_done")
        vlast_in, gate_in = sem("vlast_in"), sem("gate_in")
        pe_unit, act_unit, index_added = sem("pe_unit"), sem("act_unit"), sem("index_added")
        scanned = sem("scanned")
        pe_T, act_T, pe_pv = sem("pe_T"), sem("act_T"), sem("pe_pv")
        y_done, prod_done = sem("y_done"), sem("prod_done")
        y_hi_done, y_lo_done, y_st = sem("y_hi_done"), sem("y_lo_done"), sem("y_st")
        dve_step, mid_ready, act_count = sem("dve_step"), sem("mid_ready"), sem("act_count")
        sel_ready, sel_st = sem("sel_ready"), sem("sel_st")

        block = ctx.enter_context(nc.Block())

        def plan(s):
            j, h = s // HEADS, s % HEADS
            some = [("unit", u, 0) for u in range(first_unit[s + AHEAD], first_unit[s + AHEAD + 1])] if s < S else []
            gs = [("group", g, 0) for g in tr.by_step[s - LAG]] if LAG <= s < S + LAG + 2 else []
            counts = [("count", j, 3 * h + 1), ("count", j, 3 * h + 2)] if 0 <= s < S else []
            both = mix(some, gs)
            middle = int(len(both) * MIDDLE)
            return both[:middle] + counts[:1] + both[middle:] + counts[1:]

        def store_y(sp, j):
            for part, src in enumerate((y, prod)):
                sp.dma_start(scr["y"][part, j, :, 8:12, :],
                             src[:].rearrange("p (c q) -> p c q", c=4)).then_inc(y_st, 16)

        @block.sync
        def _(sp):
            def load_k(dst, src, a, b, s):
                for part in range(2):
                    sp.dma_start(dst[64 * part:64 * part + 64, ..., a:b].bitcast(F32),
                                 src[part, ..., a:b]).then_inc(s, 16)

            def load_q(dst, src, s, heads=slice(0, HEADS)):
                for copy in range(2):
                    sp.dma_start(dst[64 * copy:64 * copy + 64, :, heads].bitcast(F32),
                                 src[:, :, heads].rearrange("part d h q -> d part h q")).then_inc(s, 16)

            def load_qc(j, half):
                if j >= 1:
                    sp.wait_ge(pe_unit, after["stick", j - 1, 4 * half + 3])
                load_q(qc[:], scr["q_c"][j], qc_in[half], slice(4 * half, 4 * half + 4))

            def load_values(t):
                c0, n = key_tile(t)
                if t == 0:
                    sp.wait_ge(v_zero, 1)
                    sp.dma_start(vc[0:n, 0, :], scr["v_c"][0:n, :]).then_inc(v_meta_in, 16)
                    sp.dma_start(vprev[1:n, :], scr["v_c"][0:n - 1, :]).then_inc(v_meta_in, 16)
                else:
                    sp.wait_ge(v_done, t)
                    sp.dma_start(vc[:, t, :], scr["v_c"][c0:c0 + n, :]).then_inc(v_in, 16)
                    sp.dma_start(vprev[:, :], scr["v_c"][c0 - 1:c0 + n - 1, :]).then_inc(v_in, 16)

            load_q(qi[:], scr["q_i"][0], qi_in)
            load_k(ki, scr["k_i"].rearrange("a d h n -> a d (h n)"), 0, NKEY, ki_in)
            sp.dma_start(wi[:], scr["w_i"]).then_inc(const_in, 16)
            sp.dma_start(eye[:], ident).then_inc(const_in, 16)
            sp.dma_start(prod[:, 0:P], stick_mask).then_inc(const_in, 16)
            sp.dma_start(pow2[:], halves).then_inc(const_in, 16)
            load_qc(0, 0)
            load_qc(0, 1)
            load_k(kc, scr["k_c"], 0, N_META + 512, kc_in[0])
            load_values(0)
            load_values(1)
            for i in range(1, 4):
                load_k(kc, scr["k_c"], N_META + 512 * i, N_META + 512 * (i + 1), kc_in[i])
            sp.wait_ge(pe_unit, after["index", 0, HEADS - 1])
            load_q(qi[:], scr["q_i"][1], qi_in)
            for j in range(BLOCKS):
                last = block_keys(j) - 1
                if j >= 1:
                    sp.wait_ge(prod_done, j)
                sp.dma_start(gate[:], scr["gate"][j, :, 8:12, :]).then_inc(gate_in, 16)
                if j >= 1:
                    sp.wait_ge(y_hi_done, j)
                    sp.wait_ge(y_lo_done, j)
                    store_y(sp, j - 1)
                    sp.wait_ge(y_st, 32 * j)
                sp.dma_start(y[:], scr["v_c"][last:last + 1, :].partition_broadcast(P)).then_inc(vlast_in, 16)
                if j + 1 < BLOCKS:
                    load_qc(j + 1, 0)
                    load_values(j + 2)
                if j + 2 < BLOCKS:
                    sp.wait_ge(pe_unit, after["index", j + 1, HEADS - 1])
                    load_q(qi[:], scr["q_i"][j + 2], qi_in)
                if j >= 1:
                    sp.wait_ge(sel_ready, j)
                    sp.dma_start(scr["sel"][j - 1, :, 0:block_keys(j - 1)],
                                 between[:, 0:block_keys(j - 1)]).then_inc(sel_st, 16)
                if j + 1 < BLOCKS:
                    load_qc(j + 1, 1)
            sp.wait_ge(y_hi_done, BLOCKS)
            sp.wait_ge(y_lo_done, BLOCKS)
            store_y(sp, BLOCKS - 1)
            sp.wait_ge(sel_ready, BLOCKS)
            sp.dma_start(scr["sel"][BLOCKS - 1, :, :], between[:, :]).then_inc(sel_st, 16)
            sp.wait_ge(y_st, 32 * BLOCKS)
            sp.wait_ge(sel_st, 16 * BLOCKS)

        @block.gpsimd
        def _(pool):
            nc.gpsimd.memset(vprev[0:1, :], 0.0).then_inc(v_zero, 1)
            for t in range(BLOCKS + 1):
                _, n = key_tile(t)
                if t == 0:
                    pool.wait_ge(v_meta_in, 32)
                else:
                    pool.wait_ge(v_in, 32 * t)
                nc.gpsimd.tensor_tensor(vc[0:n, t, :], vprev[0:n, :], vc[0:n, t, :], ALU.subtract).then_inc(v_done, 1)

        @block.tensor
        def _(pe):
            pe.wait_ge(const_in, 64)

            def fill(u):
                kind, j, h, c0, c1 = units[u]
                if u >= SLOTS:
                    pe.wait_ge(act_unit, u - SLOTS + 1)
                if kind == "index":
                    pe.wait_ge(ki_in, 32)
                    pe.wait_ge(qi_in, 32 * (j + 1))
                    q_two, k_two = [qi[:, p, h, :] for p in range(2)], ki[:]
                else:
                    for i in range(j // 4 + 1):
                        pe.wait_ge(kc_in[i], 32)
                    pe.wait_ge(qc_in[h // 4], 32 * (j + 1))
                    q_two, k_two = [qc[:, p, h, :] for p in range(2)], kc[:, h, :]
                ins = two_pass_scores(nc, ps[:, u % SLOTS, :], q_two, k_two, c0, c1)
                own = block_keys(j) - P
                a = max(own, c0)
                if kind == "stick" and a < c1:
                    pe.wait_ge(mask_done, 2)
                    ins = nc.tensor.matmul(ps[:, u % SLOTS, a - c0:c1 - c0], eye16[:], mask[:, a - own:c1 - own],
                                           start=False, stop=True, skip_group_check=True)
                ins.then_inc(pe_unit, 1)

            def wait_copied(g):
                pe.wait_ge({"act": act_T, "gate": prod_done}[tr.copier[g]], tr.rank[g] + 1)

            def transposes(g):
                w, tiles = tr.groups[g]
                if g >= T_BANKS:
                    wait_copied(g - T_BANKS)
                bank = ps[:, SLOTS + g % T_BANKS, :]
                if tiles[0] == "out":
                    pe.wait_ge(y_done, tiles[1] + 1)
                    for c in range(4):
                        ins = nc.tensor.transpose(bank[:, P * c:P * c + P], y[:, P * c:P * c + P], eye[:])
                else:
                    pe.wait_ge(scanned, w + 1)
                    for i, t in enumerate(tiles):
                        c0, n = key_tile(t)
                        ins = nc.tensor.transpose(bank[0:n, P * i:P * i + P], rem[:, w % 3, c0:c0 + n], eye[:])
                ins.then_inc(pe_T, 1)

            def values(g):
                w, tiles = tr.groups[g]
                j, h = steps[w]
                wait_copied(g)
                pe.wait_ge(v_done, j + 2)
                if h == 0 and tiles[0] == 1 and j >= 2:
                    pe.wait_ge(y_done, j - 1)
                for i, t in enumerate(tiles):
                    _, n = key_tile(t)
                    ins = nc.tensor.matmul(ps[:, 6 + j % 2, DH * h:DH * h + DH],
                                           pT[0:n, tr.slot[g] % T_BUFS, P * i:P * i + P],
                                           vc[0:n, t, DH * h:DH * h + DH],
                                           start=(tiles[0] == 1 and i == 0), stop=(t == 0))
                ins.then_inc(pe_pv, 1)

            due = []
            for s in range(-AHEAD, S + 6):
                for what, i, _ in plan(s):
                    if what == "unit":
                        fill(i)
                    elif what == "group" and tr.copier[i] == "gate":
                        while due:
                            values(due.pop(0))
                        transposes(i)
                    elif what == "group":
                        transposes(i)
                        due.append(i)
                        if len(due) > BEHIND:
                            values(due.pop(0))

        @block.scalar
        def _(act):
            def take(u):
                kind, j, h, c0, c1 = units[u]
                act.wait_ge(pe_unit, u + 1)
                src = ps[:, u % SLOTS, :][:, 0:c1 - c0]
                if kind == "index":
                    i = n_index[u]
                    if i >= SLOTS:
                        act.wait_ge(index_added, i - SLOTS + 1)
                    nc.scalar.activation(relu[:, i % SLOTS, 0:c1 - c0], src, ACT.Relu).then_inc(act_unit, 1)
                else:
                    s = HEADS * j + h
                    if s >= 3:
                        act.wait_ge(pe_T, tr.last(s - 3) + 1)
                    nc.scalar.activation(rem[:, s % 3, c0:c1], src, ACT.Sigmoid, scale=-1.0).then_inc(act_unit, 1)

            def copy_group(g):
                w, tiles = tr.groups[g]
                if tr.copier[g] != "act":
                    return
                act.wait_ge(pe_T, g + 1)
                i = tr.slot[g]
                if i >= T_BUFS:
                    act.wait_ge(pe_pv, i - T_BUFS + 1)
                n = N_META if tiles == [0] else P
                nc.scalar.activation(pT[0:n, i % T_BUFS, 0:P * len(tiles)],
                                     ps[0:n, SLOTS + g % T_BANKS, 0:P * len(tiles)],
                                     ACT.Copy).then_inc(act_T, 1)

            def count(j, k):
                n = block_keys(j)
                act.wait_ge(mid_ready, ROUNDS * j + k + 1)
                nc.scalar.activation(junk[:, 1, 0:n], score[:, j % 3, 0:n], ACT.Sign, scale=-1.0,
                                     bias=mids[:, k:k + 1], accum_out=cnt[:, k:k + 1]).then_inc(act_count, 1)

            def high_part(j):
                act.wait_ge(prod_done, j + 1)
                nc.scalar.activation(y[:].bitcast(F32R), prod[:], ACT.Copy).then_inc(y_hi_done, 1)

            for s in range(-AHEAD, S + 6):
                j, h = s // HEADS, s % HEADS
                for what, i, k in plan(s):
                    if what == "unit":
                        take(i)
                    elif what == "group":
                        copy_group(i)
                    else:
                        count(i, k)
                if s >= HEADS and h == CLOSE + 1:
                    high_part(j - 1)

        @block.vector
        def _(dve):
            done = [0]

            def chain(ins, wait=True):
                ins.then_inc(dve_step, 1)
                done[0] += 1
                if wait:
                    dve.wait_ge(dve_step, done[0])

            chain(nc.vector.memset(zeros[:], 0.0))
            chain(nc.vector.memset(ones[:], 1.0))
            dve.wait_ge(const_in, 64)
            nc.vector.tensor_copy(eye16[:], eye[:]).then_inc(mask_done, 1)
            nc.vector.tensor_copy(mask[:], prod[:, 0:P]).then_inc(mask_done, 1)

            def add_scores(u):
                _, j, h, c0, c1 = units[u]
                i = n_index[u]
                dve.wait_ge(act_unit, u + 1)
                r, out, w = relu[:, i % SLOTS, 0:c1 - c0], score[:, j % 3, c0:c1], wi[:, j, h:h + 1]
                if h == 0:
                    ins = nc.vector.tensor_scalar(out, r, w, None, ALU.mult)
                else:
                    dve.wait_ge(index_added, n_index[after["index", j, h - 1]])
                    ins = nc.vector.scalar_tensor_tensor(out=out, in0=r, scalar=w, in1=out, op0=ALU.mult, op1=ALU.add)
                ins.then_inc(index_added, 1)

            def remainders(s):
                j, h = steps[s]
                n = block_keys(j)
                r = rem[:, s % 3, 0:n]
                dve.wait_ge(act_unit, after["stick", j, h])
                nc.vector.tensor_tensor_scan(r[:, ::-1], r[:, ::-1], zeros[:, 0:1].to_broadcast([P, n]), 1.0,
                                             ALU.mult, ALU.add).then_inc(scanned, 1)

            def score_range(j, side):
                dve.wait_ge(index_added, n_index[after["index", j, HEADS - 1]])
                chain(nc.vector.tensor_reduce(ext[:, j % 2, side:side + 1], score[:, j % 3, 0:block_keys(j)], AX_X,
                                              ALU.max if side else ALU.min))

            def open_choice(j):
                n = block_keys(j)
                e = ext[:, j % 2, :]
                chain(nc.vector.memset(score[0:64, j % 3, n - 64:n], -HUGE))
                chain(nc.vector.tensor_tensor(e[:, 2:3], e[:, 1:2], e[:, 0:1], ALU.subtract))
                chain(nc.vector.tensor_scalar(wid[:], pow2[:], e[:, 2:3], None, ALU.mult))
                ins = nc.vector.tensor_tensor(mids[:, 0:1], e[:, 0:1], wid[:, 0:1], ALU.add)
                ins.then_inc(mid_ready, 1)
                dve.wait_ge(mid_ready, ROUNDS * j + 1)

            def settle(j, k):
                n = block_keys(j)
                if k % 3:
                    dve.wait_ge(act_count, 2 * HEADS * j + k - k // 3)
                    chain(nc.vector.tensor_scalar(up[:, k:k + 1], cnt[:, k:k + 1], float(n - 2 * TOPK), 0.5,
                                                  ALU.is_le, ALU.subtract))
                else:
                    chain(nc.vector.tensor_scalar(up[:, k:k + 1], cnt[:, k:k + 1], float(TOPK), 0.5,
                                                  ALU.is_ge, ALU.subtract))
                ins = nc.vector.scalar_tensor_tensor(out=mids[:, k + 1:k + 2], in0=up[:, k:k + 1],
                                                     scalar=wid[:, k:k + 1], in1=mids[:, k:k + 1],
                                                     op0=ALU.mult, op1=ALU.add)
                if k + 1 < ROUNDS:
                    ins.then_inc(mid_ready, 1)
                    dve.wait_ge(mid_ready, ROUNDS * j + k + 2)
                else:
                    chain(ins)

            def count(j, k):
                n = block_keys(j)
                chain(nc.vector.tensor_scalar(junk[:, 0, 0:n], score[:, j % 3, 0:n], mids[:, k:k + 1], None,
                                              ALU.is_ge, ALU.add, accum_out=cnt[:, k:k + 1]))

            def bounds(j):
                e = ext[:, j % 2, :]
                settle(j, ROUNDS - 1)
                tried = mids[:, 0:ROUNDS]
                chain(nc.vector.scalar_tensor_tensor(out=cand[:, 0, :], in0=up[:], scalar=HUGE, in1=tried,
                                                     op0=ALU.mult, op1=ALU.min))
                chain(nc.vector.scalar_tensor_tensor(out=cand[:, 1, :], in0=up[:], scalar=HUGE, in1=tried,
                                                     op0=ALU.mult, op1=ALU.max))
                chain(nc.vector.tensor_reduce(e[:, 3:4], cand[:, 0, :], AX_X, ALU.max))
                chain(nc.vector.tensor_reduce(e[:, 4:5], cand[:, 1, :], AX_X, ALU.min))
                chain(nc.vector.tensor_tensor(e[:, 3:4], e[:, 3:4], e[:, 0:1], ALU.max))

            def choose(j, stage):
                n = block_keys(j)
                e = ext[:, j % 2, :]
                sc = score[:, j % 3, 0:n]
                above, mid, pos = above_hi[:, 0:n], between[:, 0:n], order[:, 0:n]
                if stage == 0:
                    chain(nc.vector.tensor_scalar(above, sc, e[:, 4:5], None, ALU.is_gt, ALU.add,
                                                  accum_out=e[:, 5:6]))
                    chain(nc.vector.tensor_scalar(e[:, 6:7], e[:, 5:6], -1.0, float(TOPK), ALU.mult, ALU.add))
                elif stage == 1:
                    if j >= 1:
                        dve.wait_ge(sel_st, 16 * j)
                    chain(nc.vector.scalar_tensor_tensor(out=mid, in0=sc, scalar=e[:, 3:4], in1=above,
                                                         op0=ALU.is_ge, op1=ALU.subtract))
                elif stage == 2:
                    chain(nc.vector.tensor_tensor_scan(pos, ones[:, 0:1].to_broadcast([P, n]), mid, 0.0,
                                                       ALU.mult, ALU.add))
                elif stage == 3:
                    chain(nc.vector.scalar_tensor_tensor(out=mid, in0=pos, scalar=e[:, 6:7], in1=mid,
                                                         op0=ALU.is_le, op1=ALU.mult))
                elif stage == 4:
                    nc.vector.scalar_tensor_tensor(out=mid, in0=mid, scalar=0.5, in1=above,
                                                   op0=ALU.subtract, op1=ALU.add).then_inc(sel_ready, 1)
                    dve.wait_ge(sel_ready, j + 1)

            def add_last(j):
                dve.wait_ge(pe_pv, tr.slot[tr.last(HEADS * j + HEADS - 1)] + 1)
                dve.wait_ge(vlast_in, 16 * (j + 1))
                nc.vector.tensor_tensor(y[:], ps[:, 6 + j % 2, :], y[:], ALU.add).then_inc(y_done, 1)

            def gated(j):
                g = [g for g, (_, t) in enumerate(tr.groups) if t == ("out", j)][0]
                dve.wait_ge(pe_T, g + 1)
                dve.wait_ge(gate_in, 16 * (j + 1))
                if j >= 1:
                    dve.wait_ge(y_st, 32 * j)
                nc.vector.tensor_tensor(prod[:], ps[:, SLOTS + g % T_BANKS, :], gate[:].rearrange("p c q -> p (c q)"),
                                        ALU.mult).then_inc(prod_done, 1)

            def low_part(j):
                dve.wait_ge(y_hi_done, j + 1)
                nc.vector.tensor_tensor(prod[:].bitcast(F32R), prod[:], y[:], ALU.subtract).then_inc(y_lo_done, 1)

            for s in range(-AHEAD, S + 6):
                j, h = s // HEADS, s % HEADS
                if 0 <= s <= S:
                    if h > 0:
                        settle(j, 3 * h - 1)
                    elif j >= 1:
                        bounds(j - 1)
                    if h == 0 and s < S:
                        open_choice(j)
                if 0 <= s < S:
                    count(j, 3 * h)
                    settle(j, 3 * h)
                if s >= HEADS and h == CLOSE + 2:
                    low_part(j - 1)
                if 1 <= s <= S:
                    remainders(s - 1)
                if 0 <= s < S:
                    settle(j, 3 * h + 1)
                if s >= HEADS and h < 5 and (s < S or h < 5):
                    choose(j - 1, h)
                for what, u, _ in plan(s):
                    if what == "unit" and units[u][0] == "index":
                        add_scores(u)
                if h >= HEADS - 2 and -2 <= s < S - HEADS:
                    score_range(j + 1, h - HEADS + 2)
                if s >= HEADS and h == CLOSE:
                    add_last(j - 1)
                if s >= HEADS and h == CLOSE + 1:
                    gated(j - 1)
BANDS = 2
BAND = N_META + 64 + P
NEAR = N_META + 64


def softmax_mixers(nc, ident, distance, band_distance, neg_slope, sinks, scr):
    STEPS = HEADS + BANDS
    S = STEPS * BLOCKS
    units, first_unit = [], []
    for s in range(S):
        j, h = divmod(s, STEPS)
        first_unit.append(len(units))
        units += [(s, c0, c1) for c0, c1 in unit_columns(j)] if h < HEADS else [(s, 0, 2), (s, 2, 4)]
    first_unit.append(len(units))
    closing = {STEPS * j + (STEPS if mixer else HEADS) - 1: 2 * j + mixer for j in range(BLOCKS) for mixer in range(2)}
    tr = Transposes([tile_groups(s // STEPS) if s % STEPS < HEADS else [["near"], ["own"]] for s in range(S)], closing)

    with ExitStack() as ctx:
        def sb(name, shape, dt=F32):
            return ctx.enter_context(nc.sbuf_tensor("a_" + name, shape, dt))

        def sem(name):
            return ctx.enter_context(nc.semaphore("a_" + name))

        ps = ctx.enter_context(nc.psum_tensor("a_ps", [P, 8, 512], F32))
        ka = sb("ka", [P, HEADS, NKEY], F32R)
        va = sb("va", [P, BLOCKS + 1, 512])
        qa = sb("qa", [P, 2, 2, HEADS, P], F32R)
        qb = sb("qb", [P, 2, HEADS, P], F32R)
        kb = sb("kb", [P, 2, KV_B, BAND], F32R)
        vb = sb("vb", [P, 2, 2, P])
        sel = sb("sel", [P, NKEY], BF16)
        dist = sb("dist", [P, NKEY])
        far = sb("far", [P, NKEY])
        band = sb("band", [P, 2, BAND])
        lg = sb("lg", [P, 3, NKEY])
        pT = sb("pT", [P, T_BUFS, 512])
        y = sb("y", [P, 2, 512])
        prod = sb("prod", [P, 2, 512])
        gate = sb("gate", [P, 8, P])
        eye = sb("eye", [P, P])
        nslope = sb("nslope", [P, HEADS])
        sink = sb("sink", [P, HEADS])
        nsink = sb("nsink", [P, HEADS])
        top = sb("top", [P, 3, 5])
        big = sb("big", [P, 3, 1])
        shift = sb("shift", [P, 3, 4])
        esink = sb("esink", [P, HEADS])
        total = sb("total", [P, 2, 2, HEADS])
        inv = sb("inv", [P, HEADS])

        const_in, ka_in, va_in = sem("const_in"), [sem(f"ka_in{i}") for i in range(4)], [sem(f"va_in{i}") for i in range(4)]
        qa_in, qb_in = [sem(f"qa_in{i}") for i in range(2)], sem("qb_in")
        kb_in, vb_in, band_in = [sem(f"kb_in{i}") for i in range(2)], [sem(f"vb_in{i}") for i in range(2)], [sem(f"band_in{i}") for i in range(2)]
        sel_in, gate_in = sem("sel_in"), sem("gate_in")
        far_done, pe_unit, dve_unit, shifted = sem("far_done"), sem("pe_unit"), sem("dve_unit"), sem("shifted")
        exp_done, pe_T, act_T, pe_pv = sem("exp_done"), sem("pe_T"), sem("act_T"), sem("pe_pv")
        y_done, prod_done = sem("y_done"), sem("prod_done")
        y_hi_done, y_lo_done, y_st = sem("y_hi_done"), sem("y_lo_done"), [sem(f"y_st{i}") for i in range(2)]
        dve_step = sem("dve_step")

        block = ctx.enter_context(nc.Block())

        def plan(s):
            some = [("unit", u) for u in range(first_unit[s], first_unit[s + 1])] if s < S else []
            gs = [("group", g) for g in tr.by_step[s - LAG]] if LAG <= s < S + LAG + 2 else []
            both = mix(some, gs)
            middle = len(both) // 2
            return both[:middle] + ([("exp", s - 1)] if 1 <= s <= S else []) + both[middle:]

        @block.sync
        def _(sp):
            def load_q(dst, src, s):
                for copy in range(2):
                    sp.dma_start(dst[64 * copy:64 * copy + 64].bitcast(F32),
                                 src.rearrange("part d h q -> d part h q")).then_inc(s, 16)

            def load_ka(i):
                a, b = (0 if i == 0 else N_META + 512 * i), N_META + 512 * (i + 1)
                for part in range(2):
                    sp.dma_start(ka[64 * part:64 * part + 64, :, a:b].bitcast(F32),
                                 scr["k_a"][part, :, :, a:b]).then_inc(ka_in[i], 16)
                if i == 0:
                    sp.dma_start(va[0:N_META, 0, :], scr["v_a"][0:N_META, :]).then_inc(va_in[0], 16)
                a = N_META + 512 * i
                sp.dma_start(va[:, 4 * i + 1:4 * i + 5, :],
                             scr["v_a"][a:a + 512, :].rearrange("(t p) n -> p t n", p=P)).then_inc(va_in[i], 16)

            def load_sel(j):
                if j >= 1:
                    sp.wait_ge(far_done, j)
                n = block_keys(j)
                sp.dma_start(sel[:, 0:n], scr["sel"][j, :, 0:n]).then_inc(sel_in, 16)

            def load_qa(j):
                if j >= 2:
                    sp.wait_ge(pe_unit, first_unit[STEPS * (j - 2) + HEADS])
                load_q(qa[:, j % 2], scr["q_a"][j], qa_in[j % 2])

            def load_window(j):
                if j >= 2:
                    sp.wait_ge(pe_pv, tr.slot[tr.last(STEPS * (j - 2) + STEPS - 1)] + 1)
                own = N_META + P * j
                near = own - 64 if j else own
                for part in range(2):
                    for at, c, n in ((0, 0, N_META), (N_META, near, 64), (NEAR, own, P)):
                        sp.dma_start(kb[64 * part:64 * part + 64, j % 2, :, at:at + n].bitcast(F32),
                                     scr["k_b"][part, :, :, c:c + n]).then_inc(kb_in[j % 2], 16)
                for at, c, n, side in ((0, 0, N_META, 0), (N_META, near, 64, 0), (0, own, P, 1)):
                    sp.dma_start(vb[at:at + n, j % 2, side, :], scr["v_b"][c:c + n, :]).then_inc(vb_in[j % 2], 16)
                sp.dma_start(band[:, j % 2, :], band_distance[j]).then_inc(band_in[j % 2], 16)

            load_qa(0)
            load_sel(0)
            sp.dma_start(dist[:], distance).then_inc(const_in, 16)
            sp.dma_start(eye[:], ident).then_inc(const_in, 16)
            sp.dma_start(nslope[:], neg_slope).then_inc(const_in, 16)
            sp.dma_start(sink[:], sinks[0].partition_broadcast(P)).then_inc(const_in, 16)
            load_ka(0)
            load_q(qb[:], scr["q_b"][0], qb_in)
            load_window(0)
            load_qa(1)
            load_window(1)
            for i in range(1, 4):
                load_ka(i)

            def store_y(c):
                j, mixer = divmod(c, 2)
                sp.wait_ge(y_hi_done, c + 1)
                sp.wait_ge(y_lo_done, c + 1)
                for part, src in enumerate((y, prod)):
                    sp.dma_start(scr["y"][part, j, :, 4 * mixer:4 * mixer + 4, :],
                                 src[:, c % 2, :].rearrange("p (c q) -> p c q", c=4)).then_inc(y_st[c % 2], 16)

            for j in range(BLOCKS):
                if j + 1 < BLOCKS:
                    load_sel(j + 1)
                if j >= 1:
                    sp.wait_ge(pe_unit, first_unit[STEPS * j])
                    load_q(qb[:], scr["q_b"][j], qb_in)
                if 1 <= j < BLOCKS - 1:
                    load_qa(j + 1)
                if j >= 1:
                    store_y(2 * j - 2)
                    sp.wait_ge(prod_done, 2 * j)
                sp.dma_start(gate[:], scr["gate"][j, :, 0:8, :]).then_inc(gate_in, 16)
                if 1 <= j < BLOCKS - 1:
                    load_window(j + 1)
                if j >= 1:
                    store_y(2 * j - 1)
            store_y(2 * BLOCKS - 2)
            store_y(2 * BLOCKS - 1)
            for i in range(2):
                sp.wait_ge(y_st[i], 32 * BLOCKS)

        @block.tensor
        def _(pe):
            pe.wait_ge(const_in, 64)

            def fill(u):
                s, c0, c1 = units[u]
                j, h = divmod(s, STEPS)
                if u >= SLOTS:
                    pe.wait_ge(dve_unit, u - SLOTS + 1)
                if h < HEADS:
                    for i in range(j // 4 + 1):
                        pe.wait_ge(ka_in[i], 32)
                    pe.wait_ge(qa_in[j % 2], 32 * (j // 2 + 1))
                    ins = two_pass_scores(nc, ps[:, u % SLOTS, :], [qa[:, j % 2, p, h, :] for p in range(2)],
                                          ka[:, h, :], c0, c1)
                else:
                    pe.wait_ge(kb_in[j % 2], 96 * (j // 2 + 1))
                    pe.wait_ge(qb_in, 32 * (j + 1))
                    for i in range(2):
                        g = 4 * (h - HEADS) + c0 + i
                        for p in range(2):
                            ins = nc.tensor.matmul(ps[:, u % SLOTS, BAND * i:BAND * i + BAND], qb[:, p, g, :],
                                                   kb[:, j % 2, g // 4, :], start=(p == 0), stop=(p == 1))
                ins.then_inc(pe_unit, 1)

            def wait_copied(g):
                pe.wait_ge({"act": act_T, "gate": prod_done}[tr.copier[g]], tr.rank[g] + 1)

            def transposes(g):
                s, tiles = tr.groups[g]
                if g >= T_BANKS:
                    wait_copied(g - T_BANKS)
                bank = ps[:, SLOTS + g % T_BANKS, :]
                if tiles[0] == "out":
                    c = tiles[1]
                    pe.wait_ge(y_done, c + 1)
                    for i in range(4):
                        ins = nc.tensor.transpose(bank[:, P * i:P * i + P], y[:, c % 2, P * i:P * i + P], eye[:])
                    ins.then_inc(pe_T, 1)
                    return
                pe.wait_ge(exp_done, s + 1)
                src = lg[:, s % 3, :]
                if tiles[0] in ("near", "own"):
                    a, n = (0, NEAR) if tiles[0] == "near" else (NEAR, P)
                    for i in range(4):
                        ins = nc.tensor.transpose(bank[0:n, P * i:P * i + P],
                                                  src[:, BAND * i + a:BAND * i + a + n], eye[:])
                else:
                    for i, t in enumerate(tiles):
                        c0, n = key_tile(t)
                        ins = nc.tensor.transpose(bank[0:n, P * i:P * i + P], src[:, c0:c0 + n], eye[:])
                ins.then_inc(pe_T, 1)

            def values(g):
                s, tiles = tr.groups[g]
                j, h = divmod(s, STEPS)
                c = 2 * j + (h >= HEADS)
                wait_copied(g)
                if h % HEADS == 0 and tiles[0] in (1, "near") and c >= 2:
                    pe.wait_ge(y_done, c - 1)
                if tiles[0] == "near":
                    return
                if tiles[0] == "own":
                    pe.wait_ge(vb_in[j % 2], 48 * (j // 2 + 1))
                    for i in range(4):
                        head = 4 * (h - HEADS) + i
                        for side, gg, n in ((0, g - 1, NEAR), (1, g, P)):
                            ins = nc.tensor.matmul(ps[:, 6 + c % 2, DH * head:DH * head + DH],
                                                   pT[0:n, tr.slot[gg] % T_BUFS, P * i:P * i + P],
                                                   vb[0:n, j % 2, side, DH * (head // 4):DH * (head // 4) + DH],
                                                   start=(side == 0), stop=(side == 1))
                    ins.then_inc(pe_pv, 2)
                    return
                for i in range(j // 4 + 1):
                    pe.wait_ge(va_in[i], 16 + 16 * (i == 0))
                for i, t in enumerate(tiles):
                    _, n = key_tile(t)
                    ins = nc.tensor.matmul(ps[:, 6 + c % 2, DH * h:DH * h + DH],
                                           pT[0:n, tr.slot[g] % T_BUFS, P * i:P * i + P],
                                           va[0:n, t, DH * h:DH * h + DH],
                                           start=(tiles[0] == 1 and i == 0), stop=(t == 0))
                ins.then_inc(pe_pv, 1)

            due = []
            for s in range(S + LAG + 2):
                for what, i in plan(s):
                    if what == "unit":
                        fill(i)
                    elif what == "group" and tr.copier[i] == "gate":
                        while due:
                            values(due.pop(0))
                        transposes(i)
                    elif what == "group":
                        transposes(i)
                        due.append(i)
                        if len(due) > BEHIND:
                            values(due.pop(0))

        @block.scalar
        def _(act):
            def exponentials(s):
                j, h = divmod(s, STEPS)
                act.wait_ge(shifted, s + 1)
                if h < HEADS:
                    row = lg[:, s % 3, 0:block_keys(j)]
                    ins = nc.scalar.activation(row, row, ACT.Exp, scale=2.0 ** -(h + 1), bias=shift[:, s % 3, 0:1],
                                               accum_out=total[:, j % 2, 0, h:h + 1])
                else:
                    a = 4 * (h - HEADS)
                    nc.scalar.activation(esink[:, a:a + 4], esink[:, a:a + 4], ACT.Exp)
                    for i in range(4):
                        row = lg[:, s % 3, BAND * i:BAND * i + BAND]
                        ins = nc.scalar.activation(row, row, ACT.Exp, scale=2.0 ** -(a + i + 1),
                                                   bias=shift[:, s % 3, i:i + 1],
                                                   accum_out=total[:, j % 2, 1, a + i:a + i + 1])
                ins.then_inc(exp_done, 1)

            def copy_group(g):
                _, tiles = tr.groups[g]
                if tr.copier[g] != "act":
                    return
                act.wait_ge(pe_T, g + 1)
                i = tr.slot[g]
                if i >= T_BUFS:
                    act.wait_ge(pe_pv, i - T_BUFS + 1)
                n = NEAR if tiles[0] == "near" else N_META if tiles == [0] else P
                w = 512 if tiles[0] in ("near", "own") else P * len(tiles)
                nc.scalar.activation(pT[0:n, i % T_BUFS, 0:w], ps[0:n, SLOTS + g % T_BANKS, 0:w],
                                     ACT.Copy).then_inc(act_T, 1)

            def high_part(c):
                act.wait_ge(prod_done, c + 1)
                nc.scalar.activation(y[:, c % 2, :].bitcast(F32R), prod[:, c % 2, :], ACT.Copy).then_inc(y_hi_done, 1)

            for s in range(S + LAG + 2):
                for what, i in plan(s):
                    if what == "exp":
                        exponentials(i)
                    elif what == "group":
                        copy_group(i)
                if s - LAG - 2 in closing:
                    high_part(closing[s - LAG - 2])

        @block.vector
        def _(dve):
            done = [0]

            def chain(ins):
                ins.then_inc(dve_step, 1)
                done[0] += 1
                dve.wait_ge(dve_step, done[0])

            dve.wait_ge(const_in, 64)
            chain(nc.vector.tensor_scalar(nsink[:], sink[:], -1.0, None, ALU.mult))

            def open_block(j):
                n = block_keys(j)
                dve.wait_ge(sel_in, 16 * (j + 1))
                nc.vector.scalar_tensor_tensor(out=far[:, 0:n], in0=sel[:, 0:n], scalar=2 * BIG,
                                               in1=dist[:, NKEY - n:NKEY], op0=ALU.mult, op1=ALU.min).then_inc(far_done, 1)
                dve.wait_ge(far_done, j + 1)

            def scores(s):
                j, h = divmod(s, STEPS)
                if s >= 3:
                    dve.wait_ge(pe_T, tr.last(s - 3) + 1)
                first, end = first_unit[s], first_unit[s + 1]
                for u in range(first, end):
                    _, c0, c1 = units[u]
                    slot = ps[:, u % SLOTS, :]
                    dve.wait_ge(pe_unit, u + 1)
                    if h < HEADS:
                        ins = nc.vector.tensor_tensor_reduce(lg[:, s % 3, c0:c1], slot[:, 0:c1 - c0], far[:, c0:c1], 1.0,
                                                             -HUGE, ALU.add, ALU.max,
                                                             top[:, s % 3, u - first:u - first + 1])
                    else:
                        dve.wait_ge(band_in[j % 2], 16 * (j // 2 + 1))
                        for i in range(c0, c1):
                            at = BAND * (i - c0)
                            ins = nc.vector.tensor_tensor_reduce(lg[:, s % 3, BAND * i:BAND * i + BAND],
                                                                 slot[:, at:at + BAND], band[:, j % 2, :], 1.0, -HUGE,
                                                                 ALU.add, ALU.max, top[:, s % 3, i:i + 1])
                    ins.then_inc(dve_unit, 1)
                dve.wait_ge(dve_unit, end)
                if h < HEADS:
                    greatest = top[:, s % 3, 0:1]
                    if end - first > 1:
                        greatest = big[:, s % 3, :]
                        chain(nc.vector.tensor_reduce(greatest, top[:, s % 3, 0:end - first], AX_X, ALU.max))
                    nc.vector.tensor_scalar(shift[:, s % 3, 0:1], greatest, -(2.0 ** -(h + 1)), None,
                                            ALU.mult).then_inc(shifted, 1)
                else:
                    a = 4 * (h - HEADS)
                    chain(nc.vector.tensor_tensor(shift[:, s % 3, :], top[:, s % 3, 0:4], nslope[:, a:a + 4], ALU.mult))
                    chain(nc.vector.tensor_tensor(shift[:, s % 3, :], shift[:, s % 3, :], nsink[:, a:a + 4], ALU.min))
                    nc.vector.tensor_tensor(esink[:, a:a + 4], shift[:, s % 3, :], sink[:, a:a + 4],
                                            ALU.add).then_inc(shifted, 1)

            def normalise(c):
                j, mixer = divmod(c, 2)
                s = STEPS * j + (STEPS if mixer else HEADS) - 1
                sums = total[:, j % 2, mixer, :]
                dve.wait_ge(exp_done, s + 1)
                if mixer:
                    chain(nc.vector.tensor_tensor(sums, sums, esink[:], ALU.add))
                chain(nc.vector.reciprocal(inv[:], sums))
                dve.wait_ge(pe_pv, tr.slot[tr.last(s)] + 1)
                if c >= 2:
                    dve.wait_ge(y_st[c % 2], 32 * (c // 2))
                nc.vector.tensor_tensor(y[:, c % 2, :].rearrange("p (h d) -> p h d", h=HEADS),
                                        ps[:, 6 + c % 2, :].rearrange("p (h d) -> p h d", h=HEADS),
                                        inv[:].rearrange("p (h a) -> p h a", a=1).to_broadcast([P, HEADS, DH]),
                                        ALU.mult).then_inc(y_done, 1)

            def gated(c):
                j, mixer = divmod(c, 2)
                g = [g for g, (_, t) in enumerate(tr.groups) if t == ("out", c)][0]
                dve.wait_ge(pe_T, g + 1)
                dve.wait_ge(gate_in, 16 * (j + 1))
                nc.vector.tensor_tensor(prod[:, c % 2, :], ps[:, SLOTS + g % T_BANKS, :],
                                        gate[:, 4 * mixer:4 * mixer + 4, :].rearrange("p c q -> p (c q)"),
                                        ALU.mult).then_inc(prod_done, 1)

            def low_part(c):
                dve.wait_ge(y_hi_done, c + 1)
                nc.vector.tensor_tensor(prod[:, c % 2, :].bitcast(F32R), prod[:, c % 2, :], y[:, c % 2, :],
                                        ALU.subtract).then_inc(y_lo_done, 1)

            for s in range(S + LAG + 3):
                if s < S:
                    if s % STEPS == 0:
                        open_block(s // STEPS)
                    scores(s)
                if s - LAG - 3 in closing:
                    low_part(closing[s - LAG - 3])
                if s - LAG - 1 in closing:
                    normalise(closing[s - LAG - 1])
                if s - LAG - 2 in closing:
                    gated(closing[s - LAG - 2])
def project_out(nc, x, w_out, final_g, scr, out):
    MT = scr["y"].shape[3]
    HALF = D_MODEL // 2
    with ExitStack() as ctx:
        def sb(name, shape, dt=F32):
            return ctx.enter_context(nc.sbuf_tensor("o_" + name, shape, dt))

        def sem(name):
            return ctx.enter_context(nc.semaphore("o_" + name))

        ps = ctx.enter_context(nc.psum_tensor("o_ps", [P, 8, 512], F32))
        w_raw = sb("w_raw", [P, 3, D_MODEL])
        w_hi = sb("w_hi", [P, MT, D_MODEL], F32R)
        w_lo = sb("w_lo", [P, MT, D_MODEL], F32R)
        yt = sb("yt", [P, 2, 2, MT, P], F32R)
        xt = sb("xt", [P, 2, D_MODEL])
        res = sb("res", [P, 2, D_MODEL])
        junk = sb("junk", [P, D_MODEL])
        g = sb("g", [P, D_MODEL])
        norm = sb("norm", [P, BLOCKS, 6])

        g_in = sem("g_in")
        w_in_sem, w_hi_done, w_lo_done = [sem(f"w_in{i}") for i in range(3)], sem("w_hi_done"), sem("w_lo_done")
        y_in, x_in = [sem(f"y_in{i}") for i in range(2)], [sem(f"x_in{i}") for i in range(2)]
        mixed, added, sq_done, ms_done = sem("mixed"), sem("added"), sem("sq_done"), sem("ms_done")
        root_done, newton, scaled = sem("root_done"), sem("newton"), sem("scaled")
        out_st = [sem(f"out_st{i}") for i in range(2)]

        block = ctx.enter_context(nc.Block())

        @block.sync
        def _(sp):
            def load_block(b):
                if b >= 2:
                    sp.wait_ge(mixed, b - 1)
                for part in range(2):
                    sp.dma_start(yt[:, b % 2, part].bitcast(F32), scr["y"][part, b]).then_inc(y_in[b % 2], 16)
                if b >= 2:
                    sp.wait_ge(added, b - 1)
                sp.dma_start(xt[:, b % 2, :], x[0, P * b:P * b + P, :]).then_inc(x_in[b % 2], 16)

            def load_w(k):
                if k >= 3:
                    sp.wait_ge(w_hi_done, k - 2)
                    sp.wait_ge(w_lo_done, k - 2)
                sp.dma_start(w_raw[:, k % 3, :], w_out[0, P * k:P * k + P, :]).then_inc(w_in_sem[k % 3], 16)

            load_w(0)
            load_w(1)
            load_block(0)
            for k in range(2, MT):
                load_w(k)
            sp.dma_start(g[:], final_g.partition_broadcast(P)).then_inc(g_in, 16)
            load_block(1)
            for b in range(BLOCKS):
                if b + 2 < BLOCKS:
                    load_block(b + 2)
                sp.wait_ge(scaled, b + 1)
                sp.dma_start(out[0, P * b:P * b + P, :], res[:, b % 2, :]).then_inc(out_st[b % 2], 16)
            for i in range(2):
                sp.wait_ge(out_st[i], 16 * (BLOCKS // 2))

        @block.tensor
        def _(pe):
            for b in range(BLOCKS):
                bank = 2 * (b % 4)
                pe.wait_ge(y_in[b % 2], 32 * (b // 2 + 1))
                if b >= 4:
                    pe.wait_ge(added, b - 3)
                for k in range(MT):
                    if b == 0:
                        pe.wait_ge(w_hi_done, k + 1)
                        pe.wait_ge(w_lo_done, k + 1)
                    for i, (yp, w) in enumerate(((0, w_hi), (0, w_lo), (1, w_hi))):
                        for c in range(2):
                            ins = nc.tensor.matmul(ps[:, bank + c, :], yt[:, b % 2, yp, k, :],
                                                   w[:, k, HALF * c:HALF * c + HALF],
                                                   start=(k == 0 and i == 0), stop=(k == MT - 1 and i == 2))
                ins.then_inc(mixed, 1)

        @block.scalar
        def _(act):
            for k in range(MT):
                act.wait_ge(w_in_sem[k % 3], 16 * (k // 3 + 1))
                nc.scalar.activation(w_hi[:, k, :], w_raw[:, k % 3, :], ACT.Copy).then_inc(w_hi_done, 1)
            for b in range(BLOCKS):
                act.wait_ge(added, b + 1)
                nc.scalar.activation(junk[:], res[:, b % 2, :], ACT.Square,
                                     accum_out=norm[:, b, 0:1]).then_inc(sq_done, 1)
                act.wait_ge(ms_done, b + 1)
                nc.scalar.activation(norm[:, b, 2:3], norm[:, b, 1:2], ACT.Sqrt).then_inc(root_done, 1)

        @block.vector
        def _(dve):
            for k in range(MT):
                dve.wait_ge(w_hi_done, k + 1)
                nc.vector.tensor_tensor(w_lo[:, k, :], w_raw[:, k % 3, :], w_hi[:, k, :].bitcast(F32),
                                        ALU.subtract).then_inc(w_lo_done, 1)
            dve.wait_ge(g_in, 16)
            for b in range(BLOCKS):
                dve.wait_ge(mixed, b + 1)
                dve.wait_ge(x_in[b % 2], 16 * (b // 2 + 1))
                if b >= 2:
                    dve.wait_ge(out_st[b % 2], 16 * (b // 2))
                bank = 2 * (b % 4)
                nc.vector.tensor_tensor(res[:, b % 2, :], ps[:, bank:bank + 2, :].rearrange("p a b -> p (a b)"),
                                        xt[:, b % 2, :], ALU.add).then_inc(added, 1)
                dve.wait_ge(sq_done, b + 1)
                nc.vector.tensor_scalar(norm[:, b, 1:2], norm[:, b, 0:1], 1.0 / D_MODEL, EPS,
                                        ALU.mult, ALU.add).then_inc(ms_done, 1)
                dve.wait_ge(root_done, b + 1)
                mean, y = norm[:, b, 1:2], norm[:, b, 3:4]
                nc.vector.reciprocal(y, norm[:, b, 2:3]).then_inc(newton, 1)
                dve.wait_ge(newton, 4 * b + 1)
                nc.vector.tensor_scalar(norm[:, b, 4:5], y, y, mean, ALU.mult, ALU.mult).then_inc(newton, 1)
                dve.wait_ge(newton, 4 * b + 2)
                nc.vector.tensor_scalar(norm[:, b, 5:6], norm[:, b, 4:5], -0.5, 1.5, ALU.mult, ALU.add).then_inc(newton, 1)
                dve.wait_ge(newton, 4 * b + 3)
                nc.vector.tensor_scalar(y, y, norm[:, b, 5:6], None, ALU.mult).then_inc(newton, 1)
                dve.wait_ge(newton, 4 * b + 4)
                nc.vector.scalar_tensor_tensor(out=res[:, b % 2, :], in0=res[:, b % 2, :], scalar=y, in1=g[:],
                                               op0=ALU.mult, op1=ALU.mult).then_inc(scaled, 1)


def scratch(nc):
    def dram(name, shape, dt=F32):
        return nc.dram_tensor("s_" + name, shape, dt, kind="Internal").ap()

    scr = {n: dram(n, (BLOCKS, 2, DH, HEADS, P)) for n in ("q_a", "q_i", "q_b", "q_c")}
    scr |= {n: dram(n, (2, DH, heads, NKEY)) for n, heads in (("k_a", HEADS), ("k_c", HEADS), ("k_i", 1), ("k_b", KV_B))}
    scr |= {n: dram(n, (NKEY, w)) for n, w in (("v_a", HEADS * DH), ("v_c", HEADS * DH), ("v_b", KV_B * DH))}
    scr["w_i"] = dram("w_i", (P, BLOCKS, HEADS))
    scr["gate"] = dram("gate", (BLOCKS, P, 12, P))
    scr["sel"] = dram("sel", (BLOCKS, P, NKEY), BF16)
    scr["y"] = dram("y", (2, BLOCKS, P, 12, P))
    return scr


def build(nc, t, out):
    scr = scratch(nc)
    project(nc, t["x"], t["meta_tokens"], t["norm_g"], t["w_in"], t["kv_norm_g"], t["w_uk"], t["w_uv"],
            t["ident"], t["q_scale"], scr)
    stick_and_select(nc, t["ident"], t["stick_mask"], t["halves"], scr)
    softmax_mixers(nc, t["ident"], t["distance"], t["band_distance"], t["neg_slope"], t["sinks"], scr)
    project_out(nc, t["x"], t["w_out"], t["final_norm_g"], scr, out)


def constants():
    f = np.float32
    r, q = np.arange(P)[:, None], np.arange(P)[None]
    slope = 2.0 ** -(np.arange(HEADS) + 1.0)
    distance = -np.abs(r - (np.arange(NKEY)[None] - (NKEY - P)))
    band = np.full((BLOCKS, P, BAND), -BIG)
    near = np.arange(-64, 0)[None]
    for j in range(BLOCKS):
        band[j, :, 0:N_META] = -(N_META + P * j + r - np.arange(N_META)[None])
        if j:
            band[j, :, N_META:NEAR] = np.where(r < 64, -np.abs(r - near), -BIG)
        band[j, :, NEAR:] = np.where((r >= 64) | (q < 64), -np.abs(r - q), -BIG)
    head = 2 * np.arange(4)[None] + (r >= 64)
    return {"ident": np.eye(P, dtype=f), "q_scale": (DH ** -0.5 / slope[head]).astype(f),
            "stick_mask": np.where(q >= r, -BIG, 0.0).astype(f),
            "halves": np.broadcast_to(2.0 ** -(np.arange(ROUNDS) + 1.0), (P, ROUNDS)).astype(f),
            "distance": distance.astype(f), "band_distance": band.astype(f),
            "neg_slope": np.broadcast_to(-slope, (P, HEADS)).astype(f)}


def kernel(x, meta_tokens, norm_g, w_in, kv_norm_g, w_uk, w_uv, sinks, w_out, final_norm_g):
    import concourse.bacc as bacc
    from concourse.bass_utils import run_bass_kernel_spmd

    given = {"x": x, "meta_tokens": meta_tokens, "norm_g": np.asarray(norm_g).reshape(KT, P).T,
             "w_in": w_in, "kv_norm_g": np.asarray(kv_norm_g).reshape(P, 1), "w_uk": w_uk, "w_uv": w_uv,
             "sinks": sinks, "w_out": w_out, "final_norm_g": final_norm_g} | constants()
    given = {k: np.ascontiguousarray(v) for k, v in given.items()}
    nc = bacc.Bacc("TRN2", target_bir_lowering=False, num_devices=1)
    t = {k: nc.dram_tensor("in_" + k, v.shape, mybir.dt.from_np(v.dtype), kind="ExternalInput").ap()
         for k, v in given.items()}
    out = nc.dram_tensor("out", (1, SEQ, D_MODEL), F32, kind="ExternalOutput").ap()
    build(nc, t, out)
    result = run_bass_kernel_spmd(nc, [{"in_" + k: v for k, v in given.items()}], core_ids=[0])
    return result.results[0]["out"]
```

```python
from contextlib import ExitStack

import concourse.bass as bass
from concourse import mybir
import numpy as np

F32 = mybir.dt.float32
F32R = mybir.dt.float32r
BF16 = mybir.dt.bfloat16
ALU = mybir.AluOpType
ACT = mybir.ActivationFunctionType
AX_X = mybir.AxisListType.X

P = 128
SEQ, D_MODEL = 2048, 1024
N_META = 16
NKEY = N_META + SEQ
BLOCKS = SEQ // P
KT = D_MODEL // P
HEADS, DH = 8, 64
KV_B = 2
TOPK = 256
EPS = 1e-6
BIG = 1e30

(C_QA, C_CKV, C_QI, C_KI, C_WI, C_GA, C_QB, C_KB, C_VB, C_GB, C_QC, C_KC, C_VC, C_GC) = (
    0, 512, 640, 1152, 1216, 1224, 1736, 2248, 2376, 2504, 3016, 3528, 4040, 4552)
D_IN = 5064

WCOLS = 264


def key_tile(t):
    return (0, N_META) if t == 0 else (N_META + P * (t - 1), P)


def block_keys(j):
    return N_META + P * (j + 1)


def mix(*lists):
    return [x for _, _, x in sorted(((i + 0.5) / len(a), n, x) for n, a in enumerate(lists) for i, x in enumerate(a))]


def early_items():
    items = [("rows", "latent", [(C_CKV, 128), (C_WI, 8), (C_VB, 128)]),
             ("cols", "k_i", C_KI, 1, 0)]
    items += [("cols", "q_i", C_QI + 256 * i, 2, 4 * i) for i in range(2)]
    items += [("rows", "v_c", [(C_VC + 256 * i, 256)]) for i in range(2)]
    return items


def late_items():
    items = [("cols", "k_c", C_KC + 128 * i, 1, 2 * i) for i in range(4)]
    items += [("cols", "q_c", C_QC + 128 * i, 1, 2 * i) for i in range(4)]
    items += [("cols", "k_b", C_KB, 1, 0)]
    items += [("cols", "q_a", C_QA + 128 * i, 1, 2 * i) for i in range(4)]
    items += [("cols", "q_b", C_QB + 128 * i, 1, 2 * i) for i in range(4)]
    items += [("cols", "gate", c + 128 * i, 1, n + i) for n, c in ((0, C_GA), (4, C_GB), (8, C_GC)) for i in range(4)]
    return items


def projection_groups(items):
    groups = []
    for i, item in enumerate(items):
        if item[0] == "rows":
            for t in range(BLOCKS + 1):
                groups.append((i, "rows", item[1], t, key_tile(t)))
        else:
            _, name, _, tiles, first = item
            for m in range(tiles):
                if name[0] == "k":
                    groups.append((i, "cols", name, m, (0, N_META)))
                for c in range(4):
                    groups.append((i, "cols", name, m, (N_META + 512 * c, 512)))
    return groups


def latent_groups():
    groups = []
    for m in range(4):
        for c in range(-1, 4):
            groups.append((-1, "k_a", "k_a", m, (0, N_META) if c < 0 else (N_META + 512 * c, 512)))
    for t in range(BLOCKS + 1):
        groups.append((-1, "v_a", "v_a", t, key_tile(t)))
    return groups


class Stores:

    def __init__(self, items, groups, scr, stages):
        self.of = [self.dmas(items, g, scr) for g in groups]
        self.has_low = [any(part for _, _, part in dmas) for dmas in self.of]
        self.lows = np.cumsum([0] + [int(b) for b in self.has_low]).tolist()
        self.high_total, self.low_total = [0] * stages, [0] * stages
        self.high_value, self.low_value = [], []
        for u, dmas in enumerate(self.of):
            for _, _, part in dmas:
                if part == 0:
                    self.high_total[u % stages] += 16
                else:
                    self.low_total[self.lows[u] % stages] += 16
            self.high_value.append(self.high_total[u % stages])
            if self.has_low[u]:
                self.low_value.append(self.low_total[self.lows[u] % stages])

    @staticmethod
    def dmas(items, group, scr):
        item, kind, name, m, (c0, n) = group
        b = (c0 - N_META) // P
        if name == "latent":
            return [(scr["v_b"][c0:c0 + n, :], (slice(0, n), slice(136, 264)), 0)]
        if name == "v_c":
            i = item - [it[1] for it in items].index("v_c")
            return [(scr["v_c"][c0:c0 + n, 256 * i:256 * i + 256], (slice(0, n), slice(0, 256)), 0)]
        if name == "v_a":
            return [(scr["v_a"][c0:c0 + n, :], (slice(0, n), slice(0, 512)), 0)]
        if name == "gate":
            return [(scr["gate"][b:b + 4, :, items[item][4] + m, :].rearrange("b p q -> p b q"),
                     (slice(0, P), slice(0, 512)), 0)]
        head = 2 * m if name == "k_a" else items[item][4] + 2 * m
        out = []
        for part in range(2):
            for k in range(1 if name == "k_i" else 2):
                rows = slice(64 * k, 64 * k + 64)
                if name[0] == "q":
                    out.append((scr[name][b:b + 4, part, :, head + k, :].rearrange("b d q -> d b q"),
                                (rows, slice(0, 512)), part))
                else:
                    out.append((scr[name][part, :, head + k, c0:c0 + n], (rows, slice(0, n)), part))
        return out


def project(nc, x, meta_tokens, norm_g, w_in, kv_norm_g, w_uk, w_uv, ident, h_hi, h_lo, scr):
    items = early_items()
    groups = projection_groups(items)
    n_rows = 2 * (BLOCKS + 1)
    groups = groups[:-n_rows] + mix(groups[-n_rows:], latent_groups())
    width = [sum(w for _, w in it[2]) if it[0] == "rows" else 128 * it[3] for it in items]
    parts = [it[2] if it[0] == "rows" else [(it[2], 128 * it[3])] for it in items]
    first_group = {}
    last_group = {}
    for u, g in enumerate(groups):
        first_group.setdefault(g[0], u)
        last_group[g[0]] = u
    BANKS = 4
    STAGES = 3
    TILES = BLOCKS + 1
    st = Stores(items, groups, scr, STAGES)
    has_low, lows = st.has_low, st.lows
    split_at = {first_group[i - 1] + 3: i for i in range(2, len(items))}
    LAST = TILES + 3

    with ExitStack() as ctx:
        def sb(name, shape, dt=F32):
            return ctx.enter_context(nc.sbuf_tensor(name, shape, dt))

        def sem(name):
            return ctx.enter_context(nc.semaphore(name))

        ps = ctx.enter_context(nc.psum_tensor("ps", [P, 8, 512], F32))
        w_raw = sb("w_raw", [P, KT, WCOLS])
        w_hi = sb("w_hi", [P, 2, KT, WCOLS], F32R)
        w_lo = sb("w_lo", [P, 2, KT, WCOLS], F32R)
        st_hi = sb("st_hi", [P, STAGES, 512])
        st_lo = sb("st_lo", [P, STAGES, 512])
        latT = sb("latT", [P, NKEY])
        wuk = sb("wuk", [P, 512])
        wuv = sb("wuv", [P, 512])
        xt = sb("xt", [P, 2, D_MODEL])
        eye = sb("eye", [P, P])
        gT = sb("gT", [P, KT])
        kvg = sb("kvg", [P, 1])
        norm = sb("norm", [P, 4, TILES])
        lnorm = sb("lnorm", [P, 4, TILES])
        newton = sb("newton", [P, 2])
        lat = sb("lat", [P, 2, P])
        wi = sb("wi", [P, TILES, HEADS])

        const_in = sem("const_in")
        x_in = [sem(f"x_in{i}") for i in range(2)]
        sq_done, ms_done, root_done = sem("sq_done"), sem("ms_done"), sem("root_done")
        inv_done, xn_done, xT_done = sem("inv_done"), sem("xn_done"), sem("xT_done")
        h_hi_done, h_lo_done = sem("h_hi_done"), sem("h_lo_done")
        w_in_sem = sem("w_in_sem")
        w_hi_done, w_lo_done = sem("w_hi_done"), sem("w_lo_done")
        grp_done, hi_out, lo_out = sem("grp_done"), sem("hi_out"), sem("lo_out")
        hi_st = [sem(f"hi_st{i}") for i in range(STAGES)]
        lo_st = [sem(f"lo_st{i}") for i in range(STAGES)]
        lsq_done, lms_done, lroot_done = sem("lsq_done"), sem("lms_done"), sem("lroot_done")
        linv_done, lat_done, latT_ps, latT_done = sem("linv_done"), sem("lat_done"), sem("latT_ps"), sem("latT_done")
        wi_done, wi_st = sem("wi_done"), sem("wi_st")

        block = ctx.enter_context(nc.Block())

        def high_scale(name):
            return DH ** -0.5 if name[0] == "q" else 1.0

        @block.sync
        def _(sp):
            for dst, src in ((eye[:], ident), (gT[:], norm_g),
                             (kvg[:], kv_norm_g),
                             (wuk[:], w_uk[0].rearrange("r h d -> r (h d)")),
                             (wuv[:], w_uv[0].rearrange("r h d -> r (h d)"))):
                sp.dma_start(dst, src).then_inc(const_in, 16)

            def load_x(t):
                c0, n = key_tile(t)
                if t >= 2:
                    sp.wait_ge(xT_done, t - 1)
                src = meta_tokens if t == 0 else x[0, P * (t - 1):P * t, :]
                sp.dma_start(xt[0:n, t % 2, :], src).then_inc(x_in[t % 2], 16)

            def load_w(i):
                if i >= 1:
                    sp.wait_ge(w_hi_done, i)
                    sp.wait_ge(w_lo_done, i)
                at = 0
                for c, w in parts[i]:
                    sp.dma_start(w_raw[:, :, at:at + w],
                                 w_in[0, :, c:c + w].rearrange("(k p) n -> p k n", p=P)).then_inc(w_in_sem, 16)
                    at += w

            def store(u):
                sp.wait_ge(hi_out, u + 1)
                if has_low[u]:
                    sp.wait_ge(lo_out, lows[u + 1])
                for dst, (rows, cols), part in st.of[u]:
                    if part == 0:
                        sp.dma_start(dst, st_hi[rows, u % STAGES, cols]).then_inc(hi_st[u % STAGES], 16)
                    else:
                        s = lows[u] % STAGES
                        sp.dma_start(dst, st_lo[rows, s, cols]).then_inc(lo_st[s], 16)

            load_x(0)
            load_w(0)
            load_x(1)
            for t in range(2, TILES):
                load_x(t)
                if t == 4:
                    load_w(1)
                if t >= 4:
                    store(t - 4)
            for u in range(TILES - 4, len(groups)):
                i = groups[u][0]
                if i >= 1 and u == first_group[i] and i + 1 < len(items):
                    load_w(i + 1)
                store(u)
                if u == TILES - 1:
                    sp.wait_ge(wi_done, TILES)
                    sp.dma_start(scr["w_i"], wi[:, 1:, :]).then_inc(wi_st, 16)
            for s in range(STAGES):
                sp.wait_ge(hi_st[s], st.high_total[s])
                sp.wait_ge(lo_st[s], st.low_total[s])
            sp.wait_ge(wi_st, 16)

        w_dmas = np.cumsum([len(p) for p in parts]).tolist()

        @block.gpsimd
        def _(pool):
            for i in range(len(items)):
                pool.wait_ge(w_in_sem, 16 * w_dmas[i])
                pool.wait_ge(w_hi_done, i + 1)
                if i >= 2:
                    pool.wait_ge(grp_done, last_group[i - 2] + 1)
                w = width[i]
                nc.gpsimd.tensor_tensor(w_lo[:, i % 2, :, 0:w], w_raw[:, :, 0:w],
                                        w_hi[:, i % 2, :, 0:w].bitcast(F32), ALU.subtract).then_inc(w_lo_done, 1)

        @block.scalar
        def _(act):
            act.wait_ge(const_in, 80)

            def split_w(i):
                act.wait_ge(w_in_sem, 16 * w_dmas[i])
                if i >= 2:
                    act.wait_ge(grp_done, last_group[i - 2] + 1)
                nc.scalar.activation(w_hi[:, i % 2, :, 0:width[i]], w_raw[:, :, 0:width[i]],
                                     ACT.Copy).then_inc(w_hi_done, 1)

            def square(t):
                _, n = key_tile(t)
                act.wait_ge(x_in[t % 2], 16 * (t // 2 + 1))
                junk = st_lo[0:n, 0:2, :].rearrange("p a b -> p (a b)")
                nc.scalar.activation(junk, xt[0:n, t % 2, :], ACT.Square,
                                     accum_out=norm[0:n, 0, t:t + 1]).then_inc(sq_done, 1)
                act.wait_ge(ms_done, t + 1)
                nc.scalar.activation(norm[0:n, 2, t:t + 1], norm[0:n, 1, t:t + 1], ACT.Sqrt).then_inc(root_done, 1)

            def h_high(t):
                c0, n = key_tile(t)
                act.wait_ge(xT_done, t + 1)
                for k in range(KT):
                    b = 2 * (t % 2) + k // 4
                    last = nc.scalar.activation(h_hi[:, k, c0:c0 + n], ps[:, b, P * (k % 4):P * (k % 4) + n],
                                                ACT.Copy, scale=gT[:, k:k + 1])
                last.then_inc(h_hi_done, 1)

            def latent_scale(t):
                c0, n = key_tile(t)
                src = ps[0:n, 4 + t % BANKS, :]
                nc.scalar.activation(st_lo[0:n, 0, 0:128], src[:, 0:128], ACT.Square,
                                     accum_out=lnorm[0:n, 0, t:t + 1]).then_inc(lsq_done, 1)
                nc.scalar.activation(wi[0:n, t, :], src[:, 128:136], ACT.Copy, scale=HEADS ** -0.5).then_inc(wi_done, 1)
                act.wait_ge(lms_done, t + 1)
                nc.scalar.activation(lnorm[0:n, 2, t:t + 1], lnorm[0:n, 1, t:t + 1], ACT.Sqrt).then_inc(lroot_done, 1)

            def latent_copy(t):
                c0, n = key_tile(t)
                act.wait_ge(latT_ps, t + 1)
                nc.scalar.activation(latT[:, c0:c0 + n], ps[:, 4 + t % BANKS, 384:384 + n], ACT.Copy,
                                     scale=kvg[:, 0:1]).then_inc(latT_done, 1)

            def high_part(u):
                i, kind, name, m, (c0, n) = groups[u]
                if u in split_at:
                    split_w(split_at[u])
                act.wait_ge(grp_done, u + 1)
                if u >= STAGES:
                    act.wait_ge(hi_st[u % STAGES], st.high_value[u - STAGES])
                    if groups[u - STAGES][2] == "latent":
                        act.wait_ge(lat_done, u - STAGES + 1)
                bank = ps[:, 4 + u % BANKS, :]
                stage = st_hi[:, u % STAGES, :]
                if name == "latent":
                    ins = nc.scalar.activation(stage[0:n, 0:264], bank[0:n, 0:264], ACT.Copy)
                elif name == "v_c":
                    ins = nc.scalar.activation(stage[0:n, 0:256], bank[0:n, 0:256], ACT.Copy)
                elif name == "v_a":
                    ins = nc.scalar.activation(stage[0:n, :], bank[0:n, :], ACT.Copy)
                else:
                    ins = nc.scalar.activation(stage[:, 0:n].bitcast(F32R), bank[:, 0:n], ACT.Copy,
                                               scale=high_scale(name))
                ins.then_inc(hi_out, 1)

            split_w(0)
            for t in range(LAST):
                if t < TILES:
                    square(t)
                if 1 <= t <= TILES:
                    h_high(t - 1)
                if 2 <= t < TILES + 2:
                    high_part(t - 2)
                    latent_scale(t - 2)
                if t >= 3:
                    latent_copy(t - 3)
            split_w(1)
            for u in range(TILES, len(groups)):
                high_part(u)

        @block.vector
        def _(dve):
            dve.wait_ge(const_in, 80)

            def mean_square(t, at, count, sq, ms):
                _, n = key_tile(t)
                dve.wait_ge(sq, t + 1)
                nc.vector.tensor_scalar(at[0:n, 1, t:t + 1], at[0:n, 0, t:t + 1], 1.0 / count, EPS,
                                        ALU.mult, ALU.add).then_inc(ms, 1)

            def inverse(t, at, root, inv):
                _, n = key_tile(t)
                dve.wait_ge(root, t + 1)
                mean, y = at[0:n, 1, t:t + 1], at[0:n, 3, t:t + 1]
                steps = 4 * t
                nc.vector.reciprocal(y, at[0:n, 2, t:t + 1]).then_inc(inv, 1)
                dve.wait_ge(inv, steps + 1)
                nc.vector.tensor_scalar(newton[0:n, 0:1], y, y, mean, ALU.mult, ALU.mult).then_inc(inv, 1)
                dve.wait_ge(inv, steps + 2)
                nc.vector.tensor_scalar(newton[0:n, 1:2], newton[0:n, 0:1], -0.5, 1.5, ALU.mult, ALU.add).then_inc(inv, 1)
                dve.wait_ge(inv, steps + 3)
                nc.vector.tensor_scalar(y, y, newton[0:n, 1:2], None, ALU.mult).then_inc(inv, 1)
                dve.wait_ge(inv, steps + 4)

            def normalise(t):
                _, n = key_tile(t)
                mean_square(t, norm, D_MODEL, sq_done, ms_done)
                inverse(t, norm, root_done, inv_done)
                nc.vector.tensor_scalar(xt[0:n, t % 2, :], xt[0:n, t % 2, :], norm[0:n, 3, t:t + 1], None,
                                        ALU.mult).then_inc(xn_done, 1)

            def h_low(t):
                c0, n = key_tile(t)
                dve.wait_ge(h_hi_done, t + 1)
                for k in range(KT):
                    b = 2 * (t % 2) + k // 4
                    last = nc.vector.scalar_tensor_tensor(
                        out=h_lo[:, k, c0:c0 + n], in0=ps[:, b, P * (k % 4):P * (k % 4) + n], scalar=gT[:, k:k + 1],
                        in1=h_hi[:, k, c0:c0 + n].bitcast(F32), op0=ALU.mult, op1=ALU.subtract)
                last.then_inc(h_lo_done, 1)

            def latent_norm(t):
                _, n = key_tile(t)
                mean_square(t, lnorm, P, lsq_done, lms_done)
                inverse(t, lnorm, lroot_done, linv_done)
                if t >= 2:
                    dve.wait_ge(latT_ps, t - 1)
                nc.vector.tensor_scalar(lat[0:n, t % 2, :], st_hi[0:n, t % STAGES, 0:128], lnorm[0:n, 3, t:t + 1],
                                        None, ALU.mult).then_inc(lat_done, 1)

            for t in range(TILES + 2):
                if t < TILES:
                    normalise(t)
                if 1 <= t <= TILES:
                    h_low(t - 1)
                if t >= 2:
                    latent_norm(t - 2)
            for u, (i, kind, name, m, (c0, n)) in enumerate(groups):
                if has_low[u]:
                    s = lows[u] % STAGES
                    dve.wait_ge(hi_out, u + 1)
                    if lows[u] >= STAGES:
                        dve.wait_ge(lo_st[s], st.low_value[lows[u] - STAGES])
                    nc.vector.scalar_tensor_tensor(
                        out=st_lo[:, s, 0:n].bitcast(F32R), in0=ps[:, 4 + u % BANKS, 0:n], scalar=high_scale(name),
                        in1=st_hi[:, u % STAGES, 0:n], op0=ALU.mult, op1=ALU.subtract).then_inc(lo_out, 1)

        @block.tensor
        def _(pe):
            pe.wait_ge(const_in, 80)

            def token_transposes(t):
                _, n = key_tile(t)
                pe.wait_ge(xn_done, t + 1)
                if t >= 2:
                    pe.wait_ge(h_hi_done, t - 1)
                    pe.wait_ge(h_lo_done, t - 1)
                for k in range(KT):
                    b = 2 * (t % 2) + k // 4
                    last = nc.tensor.transpose(ps[:, b, P * (k % 4):P * (k % 4) + n],
                                               xt[0:n, t % 2, P * k:P * k + P], eye[0:n, 0:n])
                last.then_inc(xT_done, 1)

            def latent_transpose(t):
                _, n = key_tile(t)
                pe.wait_ge(lat_done, t + 1)
                nc.tensor.transpose(ps[:, 4 + t % BANKS, 384:384 + n], lat[0:n, t % 2, :],
                                    eye[0:n, 0:n]).then_inc(latT_ps, 1)

            def products(u):
                i, kind, name, m, (c0, n) = groups[u]
                bank = ps[:, 4 + u % BANKS, :]
                if name == "latent":
                    pe.wait_ge(h_hi_done, max(m, 1) + 1)
                    pe.wait_ge(h_lo_done, max(m, 1) + 1)
                if i >= 0 and u == first_group[i]:
                    pe.wait_ge(w_hi_done, i + 1)
                    pe.wait_ge(w_lo_done, i + 1)
                if i < 0:
                    pe.wait_ge(latT_done, TILES)
                if u >= BANKS:
                    pe.wait_ge(hi_out, u - BANKS + 1)
                    if has_low[u - BANKS]:
                        pe.wait_ge(lo_out, lows[u - BANKS + 1])
                    if groups[u - BANKS][2] == "latent":
                        pe.wait_ge(latT_done, u - BANKS + 1)
                if kind in ("rows", "cols"):
                    for k in range(KT):
                        for n_pass, (wp, hp) in enumerate(((w_hi, h_hi), (w_lo, h_hi), (w_hi, h_lo))):
                            if kind == "rows":
                                out = bank[0:n, 0:width[i]]
                                still, moving = hp[:, k, c0:c0 + n], wp[:, i % 2, k, 0:width[i]]
                                if n < P:
                                    still = hp[:, k, 0:P]
                                    out = bank[:, 0:width[i]]
                            else:
                                out = bank[:, 0:n]
                                still, moving = wp[:, i % 2, k, P * m:P * m + P], hp[:, k, c0:c0 + n]
                            ins = nc.tensor.matmul(out, still, moving, start=(k == 0 and n_pass == 0),
                                                   stop=(k == KT - 1 and n_pass == 2))
                elif kind == "k_a":
                    ins = nc.tensor.matmul(bank[:, 0:n], wuk[:, P * m:P * m + P], latT[:, c0:c0 + n],
                                           start=True, stop=True)
                else:
                    ins = nc.tensor.matmul(bank[0:n, :], latT[:, c0:c0 + n], wuv[:], start=True, stop=True)
                ins.then_inc(grp_done, 1)

            for t in range(LAST):
                if t < TILES:
                    token_transposes(t)
                if t >= 3:
                    latent_transpose(t - 3)
                if t == 2:
                    products(0)
                if 2 <= t <= TILES:
                    products(t - 1)
            for u in range(TILES, len(groups)):
                products(u)


F16 = mybir.dt.float16
U8 = mybir.dt.uint8
ROUNDS = 24
UNIT = 512
HUGE = 3e38
INDEX_AT = {1: [0, 1], 2: [2], 3: [3], 4: [4], 5: [5], 6: [6, 7]}
CHOOSE_AT = {0: ([0], [1]), 2: ([2], [3]), 4: ([], [4])}


def unit_columns(j):
    n = block_keys(j)
    return [(c, min(c + UNIT, n)) for c in range(0, n, UNIT)]


def two_pass_scores(nc, out, q_two, k_two, c0, c1):
    for a in range(c0, c1, 512):
        b = min(a + 512, c1)
        for part in range(2):
            ins = nc.tensor.matmul(out[:, a - c0:b - c0], q_two[part], k_two[:, a:b],
                                   start=(part == 0), stop=(part == 1))
    return ins


def project_and_select(nc, w_in, q_scale, halves, h_hi, h_lo, scr):
    items = late_items()
    groups = projection_groups(items)
    G = len(groups)
    STAGES, RING, SLOTS, RELUS = 2, 4, 4, 3
    EVAC = 1
    st = Stores(items, groups, scr, STAGES)
    has_low, lows = st.has_low, st.lows
    first_group = [next(u for u, g in enumerate(groups) if g[0] == i) for i in range(len(items))] + [G]
    S = HEADS * BLOCKS
    TAIL = max(CHOOSE_AT) + 1
    steps = range(-1, S + TAIL)
    units, first_unit, after = [], {}, {}
    for s in steps:
        j, h = s // HEADS, s % HEADS
        first_unit[s] = len(units)
        heads = range(HEADS) if s < 0 else INDEX_AT.get(h, []) if s < S - HEADS else []
        for i in heads:
            units += [(j + 1, i, c0, c1) for c0, c1 in unit_columns(j + 1)]
            after[j + 1, i] = len(units)
    first_unit[steps[-1] + 1] = len(units)
    weight = [4 * block_keys(min(max(s // HEADS, 0), BLOCKS - 1)) + 3500 for s in steps]
    ends = np.round(np.cumsum(weight) * (G / sum(weight))).astype(int).tolist()
    group_range = {s: range(ends[k - 1] if k else 0, ends[k]) for k, s in enumerate(steps)}
    out_range = {s: range(max(g.start - EVAC, 0), max(g.stop - EVAC, 0) if s < steps[-1] else G)
                 for s, g in group_range.items()}

    PIECES = 2
    PK = KT // PIECES
    piece_at = {first_group[i - 1] - 1 + q * (4 // PIECES): (i, q) for i in range(2, len(items)) for q in range(PIECES)}

    with ExitStack() as ctx:
        def sb(name, shape, dt=F32):
            return ctx.enter_context(nc.sbuf_tensor("b_" + name, shape, dt))

        def sem(name):
            return ctx.enter_context(nc.semaphore("b_" + name))

        ps = ctx.enter_context(nc.psum_tensor("b_ps", [P, 8, 512], F32))
        w_hi = sb("w_hi", [P, 2, KT, P], F32R)
        w_lo = sb("w_lo", [P, 2, KT, P], F32R)
        w_raw = sb("w_raw", [P, PK, P])
        st_hi = sb("st_hi", [P, STAGES, 512])
        st_lo = sb("st_lo", [P, STAGES, 512])
        qs = sb("qs", [P, 4])
        ki = sb("ki", [P, NKEY], F32R)
        qi = sb("qi", [P, 2, HEADS, P], F32R)
        wi = sb("wi", [P, BLOCKS, HEADS])
        relu = sb("relu", [P, RELUS, UNIT])
        score = sb("score", [P, 2, NKEY])
        junk = sb("junk", [P, NKEY], U8)
        above_hi = sb("above_hi", [P, NKEY], U8)
        between = sb("between", [P, NKEY], BF16)
        order = sb("order", [P, NKEY], F16)
        pow2 = sb("pow2", [P, ROUNDS])
        ones = sb("ones", [P, 1])
        ext = sb("ext", [P, 2, 8])
        wid = sb("wid", [P, 2, ROUNDS])
        mids = sb("mids", [P, 2, ROUNDS + 1])
        up = sb("up", [P, 2, ROUNDS])
        cand = sb("cand", [P, ROUNDS])

        const_in, ki_in, qi_in = sem("const_in"), sem("ki_in"), sem("qi_in")
        w_in_first = [sem(f"w_in_first{i}") for i in range(2)]
        w_in_sem, w_hi_done, w_lo_done = sem("w_in"), sem("w_hi_done"), sem("w_lo_done")
        grp_done, hi_out, lo_out = sem("grp_done"), sem("hi_out"), sem("lo_out")
        hi_st = [sem(f"hi_st{i}") for i in range(STAGES)]
        lo_st = [sem(f"lo_st{i}") for i in range(STAGES)]
        pe_unit, act_unit, index_added = sem("pe_unit"), sem("act_unit"), sem("index_added")
        dve_step, mid_ready, act_count = sem("dve_step"), sem("mid_ready"), sem("act_count")
        sel_ready, sel_st = sem("sel_ready"), sem("sel_st")

        block = ctx.enter_context(nc.Block())

        def high_scale(u):
            item, _, name, _, _ = groups[u]
            if name in ("q_a", "q_b"):
                tile = items[item][4] // 2
                return qs[:, tile:tile + 1]
            return DH ** -0.5 if name[0] == "q" else 1.0

        def first_units(s):
            return range(first_unit[s], min(first_unit[s] + RELUS, first_unit[s + 1]))

        def other_units(s):
            return range(first_units(s).stop, first_unit[s + 1])

        @block.sync
        def _(sp):
            def w_rows(i, q0, q1):
                c = items[i][2]
                return w_in[0, P * PK * q0:P * PK * q1, c:c + P].rearrange("(k p) n -> p k n", p=P)

            def load_first(i):
                stage = (st_hi, st_lo)[i]
                sp.dma_start(stage[:].rearrange("p a (b n) -> p (a b) n", n=P),
                             w_rows(i, 0, PIECES)).then_inc(w_in_first[i], 16)

            def load_piece(i, q):
                sp.wait_ge(w_lo_done, PIECES * i + q)
                sp.dma_start(w_raw[:], w_rows(i, q, q + 1)).then_inc(w_in_sem, 16)

            def load_qi(j):
                if j >= 1:
                    sp.wait_ge(pe_unit, after[j - 1, HEADS - 1])
                for copy in range(2):
                    sp.dma_start(qi[64 * copy:64 * copy + 64].bitcast(F32),
                                 scr["q_i"][j].rearrange("part d h q -> d part h q")).then_inc(qi_in, 16)

            load_first(0)
            load_qi(0)
            for part in range(2):
                sp.dma_start(ki[64 * part:64 * part + 64, :].bitcast(F32), scr["k_i"][part, :, 0, :]).then_inc(ki_in, 16)
            for dst, src in ((qs[:], q_scale), (wi[:], scr["w_i"]), (pow2[:], halves)):
                sp.dma_start(dst, src).then_inc(const_in, 16)
            load_first(1)
            load_qi(1)
            for s in steps:
                j, h = s // HEADS, s % HEADS
                if h == HEADS - 1 and 0 <= j < BLOCKS - 2:
                    load_qi(j + 2)
                for u in out_range[s]:
                    if u + 1 in piece_at:
                        load_piece(*piece_at[u + 1])
                    sp.wait_ge(hi_out, u + 1)
                    if has_low[u]:
                        sp.wait_ge(lo_out, lows[u + 1])
                    for dst, (rows, cols), part in st.of[u]:
                        if part == 0:
                            sp.dma_start(dst, st_hi[rows, u % STAGES, cols]).then_inc(hi_st[u % STAGES], 16)
                        else:
                            k = lows[u] % STAGES
                            sp.dma_start(dst, st_lo[rows, k, cols]).then_inc(lo_st[k], 16)
                if s >= HEADS and h == max(CHOOSE_AT):
                    n = block_keys(j - 1)
                    sp.wait_ge(sel_ready, j)
                    sp.dma_start(scr["sel"][j - 1, :, 0:n], between[:, 0:n]).then_inc(sel_st, 16)
            for k in range(STAGES):
                sp.wait_ge(hi_st[k], st.high_total[k])
                sp.wait_ge(lo_st[k], st.low_total[k])
            sp.wait_ge(sel_st, 16 * BLOCKS)

        @block.gpsimd
        def _(pool):
            def low(i, raw, q0, q1):
                pool.wait_ge(w_hi_done, PIECES * i + q1)
                part = slice(PK * q0, PK * q1)
                nc.gpsimd.tensor_tensor(w_lo[:, i % 2, part], raw, w_hi[:, i % 2, part].bitcast(F32),
                                        ALU.subtract).then_inc(w_lo_done, q1 - q0)

            for i, stage in enumerate((st_hi, st_lo)):
                low(i, stage[:].rearrange("p a (b n) -> p (a b) n", n=P), 0, PIECES)
            for i, q in piece_at.values():
                low(i, w_raw[:], q, q + 1)

        @block.tensor
        def _(pe):
            def fill(u):
                j, h, c0, c1 = units[u]
                if u >= SLOTS:
                    pe.wait_ge(act_unit, u - SLOTS + 1)
                pe.wait_ge(ki_in, 32)
                pe.wait_ge(qi_in, 32 * (j + 1))
                two_pass_scores(nc, ps[:, u % SLOTS, :], [qi[:, p, h, :] for p in range(2)], ki[:],
                                c0, c1).then_inc(pe_unit, 1)

            def products(u):
                i, _, _, _, (c0, n) = groups[u]
                pe.wait_ge(w_lo_done, PIECES * (i + 1))
                if u >= RING:
                    pe.wait_ge(hi_out, u - RING + 1)
                    if has_low[u - RING]:
                        pe.wait_ge(lo_out, lows[u - RING + 1])
                for k in range(KT):
                    for n_pass, (w, h) in enumerate(((w_hi, h_hi), (w_lo, h_hi), (w_hi, h_lo))):
                        ins = nc.tensor.matmul(ps[:, SLOTS + u % RING, 0:n], w[:, i % 2, k, :], h[:, k, c0:c0 + n],
                                               start=(k == 0 and n_pass == 0), stop=(k == KT - 1 and n_pass == 2))
                ins.then_inc(grp_done, 1)

            for s in steps:
                for u in first_units(s):
                    fill(u)
                for u in group_range[s]:
                    products(u)
                for u in other_units(s):
                    fill(u)

        @block.scalar
        def _(act):
            act.wait_ge(const_in, 48)

            def split_first(i):
                act.wait_ge(w_in_first[i], 16)
                nc.scalar.activation(w_hi[:, i], (st_hi, st_lo)[i][:].rearrange("p a (b n) -> p (a b) n", n=P),
                                     ACT.Copy).then_inc(w_hi_done, PIECES)

            def split_piece(i, q):
                act.wait_ge(w_in_sem, 16 * (PIECES * (i - 2) + q + 1))
                act.wait_ge(grp_done, first_group[i - 1])
                nc.scalar.activation(w_hi[:, i % 2, PK * q:PK * (q + 1)], w_raw[:], ACT.Copy).then_inc(w_hi_done, 1)

            def take(u):
                _, _, c0, c1 = units[u]
                act.wait_ge(pe_unit, u + 1)
                if u >= RELUS:
                    act.wait_ge(index_added, u - RELUS + 1)
                nc.scalar.activation(relu[:, u % RELUS, 0:c1 - c0], ps[:, u % SLOTS, 0:c1 - c0],
                                     ACT.Relu).then_inc(act_unit, 1)

            def high_part(u):
                i, _, name, _, (_, n) = groups[u]
                if u in piece_at:
                    split_piece(*piece_at[u])
                act.wait_ge(grp_done, u + 1)
                if u == 0:
                    act.wait_ge(w_lo_done, 2 * PIECES)
                if u >= STAGES:
                    act.wait_ge(hi_st[u % STAGES], st.high_value[u - STAGES])
                    if has_low[u - STAGES]:
                        act.wait_ge(lo_out, lows[u - STAGES + 1])
                stage, bank = st_hi[:, u % STAGES, 0:n], ps[:, SLOTS + u % RING, 0:n]
                if name == "gate":
                    ins = nc.scalar.activation(stage, bank, ACT.Silu)
                else:
                    ins = nc.scalar.activation(stage.bitcast(F32R), bank, ACT.Copy, scale=high_scale(u))
                ins.then_inc(hi_out, 1)

            def count(j, k):
                n = block_keys(j)
                act.wait_ge(mid_ready, ROUNDS * j + k + 1)
                nc.scalar.activation(junk[:, 0:n], score[:, j % 2, 0:n], ACT.Sign, scale=-1.0,
                                     bias=mids[:, j % 2, k:k + 1], accum_out=up[:, j % 2, k:k + 1]).then_inc(act_count, 1)

            split_first(0)
            split_first(1)
            for s in steps:
                j, h = s // HEADS, s % HEADS
                for u in first_units(s):
                    take(u)
                if 0 <= s < S:
                    count(j, 3 * h + 1)
                for u in out_range[s]:
                    high_part(u)
                for u in other_units(s):
                    take(u)
                if 0 <= s < S:
                    count(j, 3 * h + 2)

        @block.vector
        def _(dve):
            done = [0]

            def chain(ins):
                ins.then_inc(dve_step, 1)
                done[0] += 1
                dve.wait_ge(dve_step, done[0])

            chain(nc.vector.memset(ones[:], 1.0))
            dve.wait_ge(const_in, 48)

            def low_part(u):
                n, k = groups[u][4][1], lows[u] % STAGES
                dve.wait_ge(hi_out, u + 1)
                if lows[u] >= STAGES:
                    dve.wait_ge(lo_st[k], st.low_value[lows[u] - STAGES])
                nc.vector.scalar_tensor_tensor(
                    out=st_lo[:, k, 0:n].bitcast(F32R), in0=ps[:, SLOTS + u % RING, 0:n], scalar=high_scale(u),
                    in1=st_hi[:, u % STAGES, 0:n], op0=ALU.mult, op1=ALU.subtract).then_inc(lo_out, 1)

            def add_scores(u):
                j, h, c0, c1 = units[u]
                dve.wait_ge(act_unit, u + 1)
                r, out, w = relu[:, u % RELUS, 0:c1 - c0], score[:, j % 2, c0:c1], wi[:, j, h:h + 1]
                if h == 0:
                    ins = nc.vector.tensor_scalar(out, r, w, None, ALU.mult)
                else:
                    dve.wait_ge(index_added, after[j, h - 1])
                    ins = nc.vector.scalar_tensor_tensor(out=out, in0=r, scalar=w, in1=out, op0=ALU.mult, op1=ALU.add)
                ins.then_inc(index_added, 1)

            def score_range(j, side):
                dve.wait_ge(index_added, after[j, HEADS - 1])
                chain(nc.vector.tensor_reduce(ext[:, j % 2, side:side + 1], score[:, j % 2, 0:block_keys(j)], AX_X,
                                              ALU.max if side else ALU.min))

            def open_choice(j):
                n = block_keys(j)
                e = ext[:, j % 2, :]
                chain(nc.vector.memset(score[0:64, j % 2, n - 64:n], -HUGE))
                chain(nc.vector.tensor_tensor(e[:, 2:3], e[:, 1:2], e[:, 0:1], ALU.subtract))
                chain(nc.vector.tensor_scalar(wid[:, j % 2], pow2[:], e[:, 2:3], None, ALU.mult))
                ins = nc.vector.tensor_tensor(mids[:, j % 2, 0:1], e[:, 0:1], wid[:, j % 2, 0:1], ALU.add)
                ins.then_inc(mid_ready, 1)
                dve.wait_ge(mid_ready, ROUNDS * j + 1)

            def settle(j, k):
                n = block_keys(j)
                if k % 3:
                    dve.wait_ge(act_count, 2 * HEADS * j + k - k // 3)
                    chain(nc.vector.tensor_scalar(up[:, j % 2, k:k + 1], up[:, j % 2, k:k + 1], float(n - 2 * TOPK), 0.5,
                                                  ALU.is_le, ALU.subtract))
                else:
                    chain(nc.vector.tensor_scalar(up[:, j % 2, k:k + 1], up[:, j % 2, k:k + 1], float(TOPK), 0.5,
                                                  ALU.is_ge, ALU.subtract))
                ins = nc.vector.scalar_tensor_tensor(out=mids[:, j % 2, k + 1:k + 2], in0=up[:, j % 2, k:k + 1],
                                                     scalar=wid[:, j % 2, k:k + 1], in1=mids[:, j % 2, k:k + 1],
                                                     op0=ALU.mult, op1=ALU.add)
                if k + 1 < ROUNDS:
                    ins.then_inc(mid_ready, 1)
                    dve.wait_ge(mid_ready, ROUNDS * j + k + 2)
                else:
                    chain(ins)

            def count(j, k):
                n = block_keys(j)
                chain(nc.vector.tensor_scalar(order[:, 0:n], score[:, j % 2, 0:n], mids[:, j % 2, k:k + 1], None,
                                              ALU.is_ge, ALU.add, accum_out=up[:, j % 2, k:k + 1]))

            def bounds(j):
                e = ext[:, j % 2, :]
                tried = mids[:, j % 2, 0:ROUNDS]
                for column, toward, best in ((3, ALU.min, ALU.max), (4, ALU.max, ALU.min)):
                    chain(nc.vector.scalar_tensor_tensor(out=cand[:], in0=up[:, j % 2], scalar=HUGE, in1=tried,
                                                         op0=ALU.mult, op1=toward))
                    chain(nc.vector.tensor_reduce(e[:, column:column + 1], cand[:], AX_X, best))
                chain(nc.vector.tensor_tensor(e[:, 3:4], e[:, 3:4], e[:, 0:1], ALU.max))

            def choose(j, stage):
                n = block_keys(j)
                e = ext[:, j % 2, :]
                sc = score[:, j % 2, 0:n]
                above, mid, pos = above_hi[:, 0:n], between[:, 0:n], order[:, 0:n]
                if stage == 0:
                    chain(nc.vector.tensor_scalar(above, sc, e[:, 4:5], None, ALU.is_gt, ALU.add,
                                                  accum_out=e[:, 5:6]))
                    chain(nc.vector.tensor_scalar(e[:, 6:7], e[:, 5:6], -1.0, float(TOPK), ALU.mult, ALU.add))
                elif stage == 1:
                    if j >= 1:
                        dve.wait_ge(sel_st, 16 * j)
                    chain(nc.vector.scalar_tensor_tensor(out=mid, in0=sc, scalar=e[:, 3:4], in1=above,
                                                         op0=ALU.is_ge, op1=ALU.subtract))
                elif stage == 2:
                    chain(nc.vector.tensor_tensor_scan(pos, ones[:, 0:1].to_broadcast([P, n]), mid, 0.0,
                                                       ALU.mult, ALU.add))
                elif stage == 3:
                    chain(nc.vector.scalar_tensor_tensor(out=mid, in0=pos, scalar=e[:, 6:7], in1=mid,
                                                         op0=ALU.is_le, op1=ALU.mult))
                elif stage == 4:
                    nc.vector.scalar_tensor_tensor(out=mid, in0=mid, scalar=0.5, in1=above,
                                                   op0=ALU.subtract, op1=ALU.add).then_inc(sel_ready, 1)
                    dve.wait_ge(sel_ready, j + 1)

            for s in steps:
                j, h = s // HEADS, s % HEADS
                prepare = h == HEADS - 1 and s < S - HEADS
                if 1 <= s <= S:
                    settle((s - 1) // HEADS, (3 * h - 1) % ROUNDS)
                if 0 <= s < S:
                    count(j, 3 * h)
                    settle(j, 3 * h)
                for u in first_units(s):
                    add_scores(u)
                if prepare and s >= 0:
                    score_range(j + 1, 0)
                beside_first, beside_second = CHOOSE_AT.get(h, ([], [])) if s >= HEADS else ([], [])
                if s >= HEADS and h == 0:
                    bounds(j - 1)
                for stage in beside_first:
                    choose(j - 1, stage)
                if 0 <= s < S:
                    settle(j, 3 * h + 1)
                for u in out_range[s]:
                    if has_low[u]:
                        low_part(u)
                for u in other_units(s):
                    add_scores(u)
                for stage in beside_second:
                    choose(j - 1, stage)
                if prepare:
                    if s < 0:
                        score_range(j + 1, 0)
                    score_range(j + 1, 1)
                    open_choice(j + 1)


LAG = 2
SLOTS = 3
T_BANKS = 3
T_BUFS = 3
LATER_KEYS = {0: 1, 1: 2, 4: 3}
BEHIND = 2


def head_steps():
    return [(j, h) for j in range(BLOCKS) for h in range(HEADS)]


def tile_groups(j):
    real = list(range(1, j + 2))
    return [real[i:i + 4] for i in range(0, len(real), 4)] + [[0]]


class Transposes:

    def __init__(self, step_tiles, closing, dve_share=0):
        self.groups, self.by_step, self.copier, self.rank, self.slot = [], [], [], [], []
        counts = {"act": 0, "dve": 0, "gate": 0}
        slots = 0
        for w in range(len(step_tiles) + 2):
            own = [(w, tiles) for tiles in (step_tiles[w] if w < len(step_tiles) else [])]
            if w - 2 in closing:
                own.append((w, ("out", closing[w - 2])))
            self.by_step.append(list(range(len(self.groups), len(self.groups) + len(own))))
            for k, g in enumerate(own):
                copier = "gate" if g[1][0] == "out" else "dve" if dve_share and k % dve_share == dve_share - 1 else "act"
                self.groups.append(g)
                self.copier.append(copier)
                self.rank.append(counts[copier])
                self.slot.append(None if copier == "gate" else slots)
                counts[copier] += 1
                slots += copier != "gate"
        self.of_slot = [g for g, n in enumerate(self.slot) if n is not None]

    def last(self, w):
        return [g for g in self.by_step[w] if self.copier[g] != "gate"][-1]


def stick_breaking(nc, ident, stick_mask, scr):
    steps = head_steps()
    S = len(steps)
    units, first_unit = [], []
    for s, (j, h) in enumerate(steps):
        first_unit.append(len(units))
        units += [(s, c0, c1) for c0, c1 in unit_columns(j)]
    first_unit.append(len(units))
    tr = Transposes([tile_groups(j) for j, _ in steps], {HEADS * j + HEADS - 1: j for j in range(BLOCKS)})

    CLOSE = LAG

    with ExitStack() as ctx:
        def sb(name, shape, dt=F32):
            return ctx.enter_context(nc.sbuf_tensor("c_" + name, shape, dt))

        def sem(name):
            return ctx.enter_context(nc.semaphore("c_" + name))

        ps = ctx.enter_context(nc.psum_tensor("c_ps", [P, 8, 512], F32))
        kc = sb("kc", [P, HEADS, NKEY], F32R)
        vc = sb("vc", [P, BLOCKS + 1, 512])
        vprev = sb("vprev", [P, 512])
        qc = sb("qc", [P, 2, HEADS, P], F32R)
        eye = sb("eye", [P, P])
        eye16 = sb("eye16", [P, P], BF16)
        mask = sb("mask", [P, P], BF16)
        rem = sb("rem", [P, 3, NKEY])
        pT = sb("pT", [P, T_BUFS, 512])
        y = sb("y", [P, 512])
        gate = sb("gate", [P, 4, P])
        prod = sb("prod", [P, 512])
        zeros = sb("zeros", [P, 1])

        mask_done, zeroed = sem("mask_done"), sem("zeroed")
        const_in, kc_in = sem("const_in"), [sem(f"kc_in{i}") for i in range(4)]
        qc_in, v_in, v_meta_in = [sem(f"qc_in{i}") for i in range(2)], sem("v_in"), sem("v_meta_in")
        v_zero, v_done = sem("v_zero"), sem("v_done")
        vlast_in, gate_in = sem("vlast_in"), sem("gate_in")
        pe_unit, act_unit = sem("pe_unit"), sem("act_unit")
        scanned = sem("scanned")
        pe_T, act_T, pe_pv = sem("pe_T"), sem("act_T"), sem("pe_pv")
        y_done, prod_done = sem("y_done"), sem("prod_done")
        y_hi_done, y_lo_done, y_st = sem("y_hi_done"), sem("y_lo_done"), sem("y_st")

        block = ctx.enter_context(nc.Block())

        def plan(s):
            some = [("unit", u) for u in range(first_unit[s], first_unit[s + 1])] if s < S else []
            gs = [("group", g) for g in tr.by_step[s - LAG]] if LAG <= s < S + LAG + 2 else []
            return mix(some, gs)

        def store_y(sp, j):
            for part, src in enumerate((y, prod)):
                sp.dma_start(scr["y"][part, j, :, 8:12, :],
                             src[:].rearrange("p (c q) -> p c q", c=4)).then_inc(y_st, 16)

        @block.sync
        def _(sp):
            def load_k(dst, src, a, b, s):
                for part in range(2):
                    sp.dma_start(dst[64 * part:64 * part + 64, ..., a:b].bitcast(F32),
                                 src[part, ..., a:b]).then_inc(s, 16)

            def load_q(dst, src, s, heads=slice(0, HEADS)):
                for copy in range(2):
                    sp.dma_start(dst[64 * copy:64 * copy + 64, :, heads].bitcast(F32),
                                 src[:, :, heads].rearrange("part d h q -> d part h q")).then_inc(s, 16)

            def load_qc(j, half):
                if j >= 1:
                    sp.wait_ge(pe_unit, first_unit[HEADS * (j - 1) + 4 * half + 4])
                load_q(qc[:], scr["q_c"][j], qc_in[half], slice(4 * half, 4 * half + 4))

            def load_values(t):
                c0, n = key_tile(t)
                if t == 0:
                    sp.wait_ge(v_zero, 1)
                    sp.dma_start(vc[0:n, 0, :], scr["v_c"][0:n, :]).then_inc(v_meta_in, 16)
                    sp.dma_start(vprev[1:n, :], scr["v_c"][0:n - 1, :]).then_inc(v_meta_in, 16)
                else:
                    sp.wait_ge(v_done, t)
                    sp.dma_start(vc[:, t, :], scr["v_c"][c0:c0 + n, :]).then_inc(v_in, 16)
                    sp.dma_start(vprev[:, :], scr["v_c"][c0 - 1:c0 + n - 1, :]).then_inc(v_in, 16)

            load_qc(0, 0)
            load_k(kc, scr["k_c"], 0, N_META + 512, kc_in[0])
            sp.dma_start(eye[:], ident).then_inc(const_in, 16)
            sp.dma_start(prod[:, 0:P], stick_mask).then_inc(const_in, 16)
            load_qc(0, 1)
            load_values(0)
            load_values(1)
            for j in range(BLOCKS):
                last = block_keys(j) - 1
                if j >= 1:
                    sp.wait_ge(prod_done, j)
                sp.dma_start(gate[:], scr["gate"][j, :, 8:12, :]).then_inc(gate_in, 16)
                if j >= 1:
                    sp.wait_ge(y_hi_done, j)
                    sp.wait_ge(y_lo_done, j)
                    store_y(sp, j - 1)
                    sp.wait_ge(y_st, 32 * j)
                sp.dma_start(y[:], scr["v_c"][last:last + 1, :].partition_broadcast(P)).then_inc(vlast_in, 16)
                if j + 1 < BLOCKS:
                    load_qc(j + 1, 0)
                    load_values(j + 2)
                if j + 1 < BLOCKS:
                    load_qc(j + 1, 1)
                if j in LATER_KEYS:
                    i = LATER_KEYS[j]
                    load_k(kc, scr["k_c"], N_META + 512 * i, N_META + 512 * (i + 1), kc_in[i])
            sp.wait_ge(y_hi_done, BLOCKS)
            sp.wait_ge(y_lo_done, BLOCKS)
            store_y(sp, BLOCKS - 1)
            sp.wait_ge(y_st, 32 * BLOCKS)

        @block.gpsimd
        def _(pool):
            nc.gpsimd.memset(vprev[0:1, :], 0.0).then_inc(v_zero, 1)
            for t in range(BLOCKS + 1):
                _, n = key_tile(t)
                if t == 0:
                    pool.wait_ge(v_meta_in, 32)
                else:
                    pool.wait_ge(v_in, 32 * t)
                nc.gpsimd.tensor_tensor(vc[0:n, t, :], vprev[0:n, :], vc[0:n, t, :], ALU.subtract).then_inc(v_done, 1)

        @block.tensor
        def _(pe):
            pe.wait_ge(const_in, 32)

            def fill(u):
                s, c0, c1 = units[u]
                j, h = steps[s]
                if u >= SLOTS:
                    pe.wait_ge(act_unit, u - SLOTS + 1)
                for i in range(j // 4 + 1):
                    pe.wait_ge(kc_in[i], 32)
                pe.wait_ge(qc_in[h // 4], 32 * (j + 1))
                ins = two_pass_scores(nc, ps[:, u % SLOTS, :], [qc[:, p, h, :] for p in range(2)], kc[:, h, :], c0, c1)
                own = block_keys(j) - P
                a = max(own, c0)
                if a < c1:
                    pe.wait_ge(mask_done, 2)
                    ins = nc.tensor.matmul(ps[:, u % SLOTS, a - c0:c1 - c0], eye16[:], mask[:, a - own:c1 - own],
                                           start=False, stop=True, skip_group_check=True)
                ins.then_inc(pe_unit, 1)

            def wait_copied(g):
                pe.wait_ge({"act": act_T, "gate": prod_done}[tr.copier[g]], tr.rank[g] + 1)

            def transposes(g):
                w, tiles = tr.groups[g]
                if g >= T_BANKS:
                    wait_copied(g - T_BANKS)
                bank = ps[:, SLOTS + g % T_BANKS, :]
                if tiles[0] == "out":
                    pe.wait_ge(y_done, tiles[1] + 1)
                    for c in range(4):
                        ins = nc.tensor.transpose(bank[:, P * c:P * c + P], y[:, P * c:P * c + P], eye[:])
                else:
                    pe.wait_ge(scanned, w + 1)
                    for i, t in enumerate(tiles):
                        c0, n = key_tile(t)
                        ins = nc.tensor.transpose(bank[0:n, P * i:P * i + P], rem[:, w % 3, c0:c0 + n], eye[:])
                ins.then_inc(pe_T, 1)

            def values(g):
                w, tiles = tr.groups[g]
                j, h = steps[w]
                wait_copied(g)
                pe.wait_ge(v_done, j + 2)
                if h == 0 and tiles[0] == 1 and j >= 2:
                    pe.wait_ge(y_done, j - 1)
                for i, t in enumerate(tiles):
                    _, n = key_tile(t)
                    ins = nc.tensor.matmul(ps[:, 6 + j % 2, DH * h:DH * h + DH],
                                           pT[0:n, tr.slot[g] % T_BUFS, P * i:P * i + P],
                                           vc[0:n, t, DH * h:DH * h + DH],
                                           start=(tiles[0] == 1 and i == 0), stop=(t == 0))
                ins.then_inc(pe_pv, 1)

            due = []
            for s in range(S + 6):
                for what, i in plan(s):
                    if what == "unit":
                        fill(i)
                    elif what == "group" and tr.copier[i] == "gate":
                        while due:
                            values(due.pop(0))
                        transposes(i)
                    elif what == "group":
                        transposes(i)
                        due.append(i)
                        if len(due) > BEHIND:
                            values(due.pop(0))

        @block.scalar
        def _(act):
            def take(u):
                s, c0, c1 = units[u]
                j, h = steps[s]
                act.wait_ge(pe_unit, u + 1)
                if s >= 3:
                    act.wait_ge(pe_T, tr.last(s - 3) + 1)
                nc.scalar.activation(rem[:, s % 3, c0:c1], ps[:, u % SLOTS, 0:c1 - c0], ACT.Sigmoid,
                                     scale=-1.0).then_inc(act_unit, 1)

            def copy_group(g):
                w, tiles = tr.groups[g]
                if tr.copier[g] != "act":
                    return
                act.wait_ge(pe_T, g + 1)
                i = tr.slot[g]
                if i >= T_BUFS:
                    act.wait_ge(pe_pv, i - T_BUFS + 1)
                n = N_META if tiles == [0] else P
                nc.scalar.activation(pT[0:n, i % T_BUFS, 0:P * len(tiles)],
                                     ps[0:n, SLOTS + g % T_BANKS, 0:P * len(tiles)],
                                     ACT.Copy).then_inc(act_T, 1)

            def high_part(j):
                act.wait_ge(prod_done, j + 1)
                nc.scalar.activation(y[:].bitcast(F32R), prod[:], ACT.Copy).then_inc(y_hi_done, 1)

            for s in range(S + 6):
                j, h = s // HEADS, s % HEADS
                for what, i in plan(s):
                    if what == "unit":
                        take(i)
                    else:
                        copy_group(i)
                if s >= HEADS and h == CLOSE + 1:
                    high_part(j - 1)

        @block.vector
        def _(dve):
            nc.vector.memset(zeros[:], 0.0).then_inc(zeroed, 1)
            dve.wait_ge(const_in, 32)
            nc.vector.tensor_copy(eye16[:], eye[:]).then_inc(mask_done, 1)
            nc.vector.tensor_copy(mask[:], prod[:, 0:P]).then_inc(mask_done, 1)

            def remainders(s):
                j, h = steps[s]
                n = block_keys(j)
                r = rem[:, s % 3, 0:n]
                dve.wait_ge(act_unit, first_unit[s + 1])
                dve.wait_ge(zeroed, 1)
                nc.vector.tensor_tensor_scan(r[:, ::-1], r[:, ::-1], zeros[:, 0:1].to_broadcast([P, n]), 1.0,
                                             ALU.mult, ALU.add).then_inc(scanned, 1)

            def add_last(j):
                dve.wait_ge(pe_pv, tr.slot[tr.last(HEADS * j + HEADS - 1)] + 1)
                dve.wait_ge(vlast_in, 16 * (j + 1))
                nc.vector.tensor_tensor(y[:], ps[:, 6 + j % 2, :], y[:], ALU.add).then_inc(y_done, 1)

            def gated(j):
                g = [g for g, (_, t) in enumerate(tr.groups) if t == ("out", j)][0]
                dve.wait_ge(pe_T, g + 1)
                dve.wait_ge(gate_in, 16 * (j + 1))
                if j >= 1:
                    dve.wait_ge(y_st, 32 * j)
                nc.vector.tensor_tensor(prod[:], ps[:, SLOTS + g % T_BANKS, :], gate[:].rearrange("p c q -> p (c q)"),
                                        ALU.mult).then_inc(prod_done, 1)

            def low_part(j):
                dve.wait_ge(y_hi_done, j + 1)
                nc.vector.tensor_tensor(prod[:].bitcast(F32R), prod[:], y[:], ALU.subtract).then_inc(y_lo_done, 1)

            for s in range(S + 6):
                j, h = divmod(s, HEADS)
                if s >= HEADS and h == CLOSE + 2:
                    low_part(j - 1)
                if 1 <= s <= S:
                    remainders(s - 1)
                if s >= HEADS and h == CLOSE:
                    add_last(j - 1)
                if s >= HEADS and h == CLOSE + 1:
                    gated(j - 1)


BANDS = 2
BAND = N_META + 64 + P
NEAR = N_META + 64


def softmax_mixers(nc, ident, distance, band_distance, neg_slope, sinks, scr):
    STEPS = HEADS + BANDS
    S = STEPS * BLOCKS
    units, first_unit = [], []
    for s in range(S):
        j, h = divmod(s, STEPS)
        first_unit.append(len(units))
        units += [(s, c0, c1) for c0, c1 in unit_columns(j)] if h < HEADS else [(s, 0, 2), (s, 2, 4)]
    first_unit.append(len(units))
    closing = {STEPS * j + (STEPS if mixer else HEADS) - 1: 2 * j + mixer for j in range(BLOCKS) for mixer in range(2)}
    tr = Transposes([tile_groups(s // STEPS) if s % STEPS < HEADS else [["near"], ["own"]] for s in range(S)], closing)

    with ExitStack() as ctx:
        def sb(name, shape, dt=F32):
            return ctx.enter_context(nc.sbuf_tensor("a_" + name, shape, dt))

        def sem(name):
            return ctx.enter_context(nc.semaphore("a_" + name))

        ps = ctx.enter_context(nc.psum_tensor("a_ps", [P, 8, 512], F32))
        ka = sb("ka", [P, HEADS, NKEY], F32R)
        va = sb("va", [P, BLOCKS + 1, 512])
        qa = sb("qa", [P, 2, 2, HEADS, P], F32R)
        qb = sb("qb", [P, 2, HEADS, P], F32R)
        kb = sb("kb", [P, 2, KV_B, BAND], F32R)
        vb = sb("vb", [P, 2, 2, P])
        sel = sb("sel", [P, NKEY], BF16)
        dist = sb("dist", [P, NKEY])
        far = sb("far", [P, NKEY])
        band = sb("band", [P, 2, BAND])
        lg = sb("lg", [P, 3, NKEY])
        pT = sb("pT", [P, T_BUFS, 512])
        y = sb("y", [P, 2, 512])
        prod = sb("prod", [P, 2, 512])
        gate = sb("gate", [P, 8, P])
        eye = sb("eye", [P, P])
        nslope = sb("nslope", [P, HEADS])
        sink = sb("sink", [P, HEADS])
        nsink = sb("nsink", [P, HEADS])
        top = sb("top", [P, 3, 5])
        big = sb("big", [P, 3, 1])
        shift = sb("shift", [P, 3, 4])
        esink = sb("esink", [P, HEADS])
        total = sb("total", [P, 2, 2, HEADS])
        inv = sb("inv", [P, HEADS])

        const_in, ka_in, va_in = sem("const_in"), [sem(f"ka_in{i}") for i in range(4)], [sem(f"va_in{i}") for i in range(4)]
        qa_in, qb_in = [sem(f"qa_in{i}") for i in range(2)], sem("qb_in")
        kb_in, vb_in, band_in = [sem(f"kb_in{i}") for i in range(2)], [sem(f"vb_in{i}") for i in range(2)], [sem(f"band_in{i}") for i in range(2)]
        sel_in, gate_in = sem("sel_in"), sem("gate_in")
        far_done, pe_unit, dve_unit, shifted = sem("far_done"), sem("pe_unit"), sem("dve_unit"), sem("shifted")
        exp_done, pe_T, act_T, pe_pv = sem("exp_done"), sem("pe_T"), sem("act_T"), sem("pe_pv")
        y_done, prod_done = sem("y_done"), sem("prod_done")
        y_hi_done, y_lo_done, y_st = sem("y_hi_done"), sem("y_lo_done"), [sem(f"y_st{i}") for i in range(2)]
        dve_step = sem("dve_step")

        block = ctx.enter_context(nc.Block())

        def plan(s):
            some = [("unit", u) for u in range(first_unit[s], first_unit[s + 1])] if s < S else []
            gs = [("group", g) for g in tr.by_step[s - LAG]] if LAG <= s < S + LAG + 2 else []
            both = mix(some, gs)
            middle = len(both) // 2
            return both[:middle] + ([("exp", s - 1)] if 1 <= s <= S else []) + both[middle:]

        @block.sync
        def _(sp):
            def load_q(dst, src, s):
                for copy in range(2):
                    sp.dma_start(dst[64 * copy:64 * copy + 64].bitcast(F32),
                                 src.rearrange("part d h q -> d part h q")).then_inc(s, 16)

            def load_ka(i):
                a, b = (0 if i == 0 else N_META + 512 * i), N_META + 512 * (i + 1)
                for part in range(2):
                    sp.dma_start(ka[64 * part:64 * part + 64, :, a:b].bitcast(F32),
                                 scr["k_a"][part, :, :, a:b]).then_inc(ka_in[i], 16)
                if i == 0:
                    sp.dma_start(va[0:N_META, 0, :], scr["v_a"][0:N_META, :]).then_inc(va_in[0], 16)
                a = N_META + 512 * i
                sp.dma_start(va[:, 4 * i + 1:4 * i + 5, :],
                             scr["v_a"][a:a + 512, :].rearrange("(t p) n -> p t n", p=P)).then_inc(va_in[i], 16)

            def load_sel(j):
                if j >= 1:
                    sp.wait_ge(far_done, j)
                n = block_keys(j)
                sp.dma_start(sel[:, 0:n], scr["sel"][j, :, 0:n]).then_inc(sel_in, 16)

            def load_qa(j):
                if j >= 2:
                    sp.wait_ge(pe_unit, first_unit[STEPS * (j - 2) + HEADS])
                load_q(qa[:, j % 2], scr["q_a"][j], qa_in[j % 2])

            def load_window(j):
                if j >= 2:
                    sp.wait_ge(pe_pv, tr.slot[tr.last(STEPS * (j - 2) + STEPS - 1)] + 1)
                own = N_META + P * j
                near = own - 64 if j else own
                for part in range(2):
                    for at, c, n in ((0, 0, N_META), (N_META, near, 64), (NEAR, own, P)):
                        sp.dma_start(kb[64 * part:64 * part + 64, j % 2, :, at:at + n].bitcast(F32),
                                     scr["k_b"][part, :, :, c:c + n]).then_inc(kb_in[j % 2], 16)
                for at, c, n, side in ((0, 0, N_META, 0), (N_META, near, 64, 0), (0, own, P, 1)):
                    sp.dma_start(vb[at:at + n, j % 2, side, :], scr["v_b"][c:c + n, :]).then_inc(vb_in[j % 2], 16)
                sp.dma_start(band[:, j % 2, :], band_distance[j]).then_inc(band_in[j % 2], 16)

            load_qa(0)
            load_sel(0)
            sp.dma_start(dist[:], distance).then_inc(const_in, 16)
            sp.dma_start(eye[:], ident).then_inc(const_in, 16)
            sp.dma_start(nslope[:], neg_slope).then_inc(const_in, 16)
            sp.dma_start(sink[:], sinks[0].partition_broadcast(P)).then_inc(const_in, 16)
            load_ka(0)
            load_q(qb[:], scr["q_b"][0], qb_in)
            load_window(0)
            load_qa(1)
            load_window(1)

            def store_y(c):
                j, mixer = divmod(c, 2)
                sp.wait_ge(y_hi_done, c + 1)
                sp.wait_ge(y_lo_done, c + 1)
                for part, src in enumerate((y, prod)):
                    sp.dma_start(scr["y"][part, j, :, 4 * mixer:4 * mixer + 4, :],
                                 src[:, c % 2, :].rearrange("p (c q) -> p c q", c=4)).then_inc(y_st[c % 2], 16)

            for j in range(BLOCKS):
                if j + 1 < BLOCKS:
                    load_sel(j + 1)
                if j >= 1:
                    sp.wait_ge(pe_unit, first_unit[STEPS * j])
                    load_q(qb[:], scr["q_b"][j], qb_in)
                if 1 <= j < BLOCKS - 1:
                    load_qa(j + 1)
                if j >= 1:
                    store_y(2 * j - 2)
                    sp.wait_ge(prod_done, 2 * j)
                sp.dma_start(gate[:], scr["gate"][j, :, 0:8, :]).then_inc(gate_in, 16)
                if 1 <= j < BLOCKS - 1:
                    load_window(j + 1)
                if j >= 1:
                    store_y(2 * j - 1)
                if j in LATER_KEYS:
                    load_ka(LATER_KEYS[j])
            store_y(2 * BLOCKS - 2)
            store_y(2 * BLOCKS - 1)
            for i in range(2):
                sp.wait_ge(y_st[i], 32 * BLOCKS)

        @block.tensor
        def _(pe):
            pe.wait_ge(const_in, 64)

            def fill(u):
                s, c0, c1 = units[u]
                j, h = divmod(s, STEPS)
                if u >= SLOTS:
                    pe.wait_ge(dve_unit, u - SLOTS + 1)
                if h < HEADS:
                    for i in range(j // 4 + 1):
                        pe.wait_ge(ka_in[i], 32)
                    pe.wait_ge(qa_in[j % 2], 32 * (j // 2 + 1))
                    ins = two_pass_scores(nc, ps[:, u % SLOTS, :], [qa[:, j % 2, p, h, :] for p in range(2)],
                                          ka[:, h, :], c0, c1)
                else:
                    pe.wait_ge(kb_in[j % 2], 96 * (j // 2 + 1))
                    pe.wait_ge(qb_in, 32 * (j + 1))
                    for i in range(2):
                        g = 4 * (h - HEADS) + c0 + i
                        for p in range(2):
                            ins = nc.tensor.matmul(ps[:, u % SLOTS, BAND * i:BAND * i + BAND], qb[:, p, g, :],
                                                   kb[:, j % 2, g // 4, :], start=(p == 0), stop=(p == 1))
                ins.then_inc(pe_unit, 1)

            def wait_copied(g):
                pe.wait_ge({"act": act_T, "gate": prod_done}[tr.copier[g]], tr.rank[g] + 1)

            def transposes(g):
                s, tiles = tr.groups[g]
                if g >= T_BANKS:
                    wait_copied(g - T_BANKS)
                bank = ps[:, SLOTS + g % T_BANKS, :]
                if tiles[0] == "out":
                    c = tiles[1]
                    pe.wait_ge(y_done, c + 1)
                    for i in range(4):
                        ins = nc.tensor.transpose(bank[:, P * i:P * i + P], y[:, c % 2, P * i:P * i + P], eye[:])
                    ins.then_inc(pe_T, 1)
                    return
                pe.wait_ge(exp_done, s + 1)
                src = lg[:, s % 3, :]
                if tiles[0] in ("near", "own"):
                    a, n = (0, NEAR) if tiles[0] == "near" else (NEAR, P)
                    for i in range(4):
                        ins = nc.tensor.transpose(bank[0:n, P * i:P * i + P],
                                                  src[:, BAND * i + a:BAND * i + a + n], eye[:])
                else:
                    for i, t in enumerate(tiles):
                        c0, n = key_tile(t)
                        ins = nc.tensor.transpose(bank[0:n, P * i:P * i + P], src[:, c0:c0 + n], eye[:])
                ins.then_inc(pe_T, 1)

            def values(g):
                s, tiles = tr.groups[g]
                j, h = divmod(s, STEPS)
                c = 2 * j + (h >= HEADS)
                wait_copied(g)
                if h % HEADS == 0 and tiles[0] in (1, "near") and c >= 2:
                    pe.wait_ge(y_done, c - 1)
                if tiles[0] == "near":
                    return
                if tiles[0] == "own":
                    pe.wait_ge(vb_in[j % 2], 48 * (j // 2 + 1))
                    for i in range(4):
                        head = 4 * (h - HEADS) + i
                        for side, gg, n in ((0, g - 1, NEAR), (1, g, P)):
                            ins = nc.tensor.matmul(ps[:, 6 + c % 2, DH * head:DH * head + DH],
                                                   pT[0:n, tr.slot[gg] % T_BUFS, P * i:P * i + P],
                                                   vb[0:n, j % 2, side, DH * (head // 4):DH * (head // 4) + DH],
                                                   start=(side == 0), stop=(side == 1))
                    ins.then_inc(pe_pv, 2)
                    return
                for i in range(j // 4 + 1):
                    pe.wait_ge(va_in[i], 16 + 16 * (i == 0))
                for i, t in enumerate(tiles):
                    _, n = key_tile(t)
                    ins = nc.tensor.matmul(ps[:, 6 + c % 2, DH * h:DH * h + DH],
                                           pT[0:n, tr.slot[g] % T_BUFS, P * i:P * i + P],
                                           va[0:n, t, DH * h:DH * h + DH],
                                           start=(tiles[0] == 1 and i == 0), stop=(t == 0))
                ins.then_inc(pe_pv, 1)

            due = []
            for s in range(S + LAG + 2):
                for what, i in plan(s):
                    if what == "unit":
                        fill(i)
                    elif what == "group" and tr.copier[i] == "gate":
                        while due:
                            values(due.pop(0))
                        transposes(i)
                    elif what == "group":
                        transposes(i)
                        due.append(i)
                        if len(due) > BEHIND:
                            values(due.pop(0))

        @block.scalar
        def _(act):
            def exponentials(s):
                j, h = divmod(s, STEPS)
                act.wait_ge(shifted, s + 1)
                if h < HEADS:
                    row = lg[:, s % 3, 0:block_keys(j)]
                    ins = nc.scalar.activation(row, row, ACT.Exp, scale=2.0 ** -(h + 1), bias=shift[:, s % 3, 0:1],
                                               accum_out=total[:, j % 2, 0, h:h + 1])
                else:
                    a = 4 * (h - HEADS)
                    nc.scalar.activation(esink[:, a:a + 4], esink[:, a:a + 4], ACT.Exp)
                    for i in range(4):
                        row = lg[:, s % 3, BAND * i:BAND * i + BAND]
                        ins = nc.scalar.activation(row, row, ACT.Exp, scale=2.0 ** -(a + i + 1),
                                                   bias=shift[:, s % 3, i:i + 1],
                                                   accum_out=total[:, j % 2, 1, a + i:a + i + 1])
                ins.then_inc(exp_done, 1)

            def copy_group(g):
                _, tiles = tr.groups[g]
                if tr.copier[g] != "act":
                    return
                act.wait_ge(pe_T, g + 1)
                i = tr.slot[g]
                if i >= T_BUFS:
                    act.wait_ge(pe_pv, i - T_BUFS + 1)
                n = NEAR if tiles[0] == "near" else N_META if tiles == [0] else P
                w = 512 if tiles[0] in ("near", "own") else P * len(tiles)
                nc.scalar.activation(pT[0:n, i % T_BUFS, 0:w], ps[0:n, SLOTS + g % T_BANKS, 0:w],
                                     ACT.Copy).then_inc(act_T, 1)

            def high_part(c):
                act.wait_ge(prod_done, c + 1)
                nc.scalar.activation(y[:, c % 2, :].bitcast(F32R), prod[:, c % 2, :], ACT.Copy).then_inc(y_hi_done, 1)

            for s in range(S + LAG + 2):
                for what, i in plan(s):
                    if what == "exp":
                        exponentials(i)
                    elif what == "group":
                        copy_group(i)
                if s - LAG - 2 in closing:
                    high_part(closing[s - LAG - 2])

        @block.vector
        def _(dve):
            done = [0]

            def chain(ins):
                ins.then_inc(dve_step, 1)
                done[0] += 1
                dve.wait_ge(dve_step, done[0])

            dve.wait_ge(const_in, 64)
            chain(nc.vector.tensor_scalar(nsink[:], sink[:], -1.0, None, ALU.mult))

            def open_block(j):
                n = block_keys(j)
                dve.wait_ge(sel_in, 16 * (j + 1))
                nc.vector.scalar_tensor_tensor(out=far[:, 0:n], in0=sel[:, 0:n], scalar=2 * BIG,
                                               in1=dist[:, NKEY - n:NKEY], op0=ALU.mult, op1=ALU.min).then_inc(far_done, 1)
                dve.wait_ge(far_done, j + 1)

            def scores(s):
                j, h = divmod(s, STEPS)
                if s >= 3:
                    dve.wait_ge(pe_T, tr.last(s - 3) + 1)
                first, end = first_unit[s], first_unit[s + 1]
                for u in range(first, end):
                    _, c0, c1 = units[u]
                    slot = ps[:, u % SLOTS, :]
                    dve.wait_ge(pe_unit, u + 1)
                    if h < HEADS:
                        ins = nc.vector.tensor_tensor_reduce(lg[:, s % 3, c0:c1], slot[:, 0:c1 - c0], far[:, c0:c1], 1.0,
                                                             -HUGE, ALU.add, ALU.max,
                                                             top[:, s % 3, u - first:u - first + 1])
                    else:
                        dve.wait_ge(band_in[j % 2], 16 * (j // 2 + 1))
                        for i in range(c0, c1):
                            at = BAND * (i - c0)
                            ins = nc.vector.tensor_tensor_reduce(lg[:, s % 3, BAND * i:BAND * i + BAND],
                                                                 slot[:, at:at + BAND], band[:, j % 2, :], 1.0, -HUGE,
                                                                 ALU.add, ALU.max, top[:, s % 3, i:i + 1])
                    ins.then_inc(dve_unit, 1)
                dve.wait_ge(dve_unit, end)
                if h < HEADS:
                    greatest = top[:, s % 3, 0:1]
                    if end - first > 1:
                        greatest = big[:, s % 3, :]
                        chain(nc.vector.tensor_reduce(greatest, top[:, s % 3, 0:end - first], AX_X, ALU.max))
                    nc.vector.tensor_scalar(shift[:, s % 3, 0:1], greatest, -(2.0 ** -(h + 1)), None,
                                            ALU.mult).then_inc(shifted, 1)
                else:
                    a = 4 * (h - HEADS)
                    chain(nc.vector.tensor_tensor(shift[:, s % 3, :], top[:, s % 3, 0:4], nslope[:, a:a + 4], ALU.mult))
                    chain(nc.vector.tensor_tensor(shift[:, s % 3, :], shift[:, s % 3, :], nsink[:, a:a + 4], ALU.min))
                    nc.vector.tensor_tensor(esink[:, a:a + 4], shift[:, s % 3, :], sink[:, a:a + 4],
                                            ALU.add).then_inc(shifted, 1)

            def normalise(c):
                j, mixer = divmod(c, 2)
                s = STEPS * j + (STEPS if mixer else HEADS) - 1
                sums = total[:, j % 2, mixer, :]
                dve.wait_ge(exp_done, s + 1)
                if mixer:
                    chain(nc.vector.tensor_tensor(sums, sums, esink[:], ALU.add))
                chain(nc.vector.reciprocal(inv[:], sums))
                dve.wait_ge(pe_pv, tr.slot[tr.last(s)] + 1)
                if c >= 2:
                    dve.wait_ge(y_st[c % 2], 32 * (c // 2))
                nc.vector.tensor_tensor(y[:, c % 2, :].rearrange("p (h d) -> p h d", h=HEADS),
                                        ps[:, 6 + c % 2, :].rearrange("p (h d) -> p h d", h=HEADS),
                                        inv[:].rearrange("p (h a) -> p h a", a=1).to_broadcast([P, HEADS, DH]),
                                        ALU.mult).then_inc(y_done, 1)

            def gated(c):
                j, mixer = divmod(c, 2)
                g = [g for g, (_, t) in enumerate(tr.groups) if t == ("out", c)][0]
                dve.wait_ge(pe_T, g + 1)
                dve.wait_ge(gate_in, 16 * (j + 1))
                nc.vector.tensor_tensor(prod[:, c % 2, :], ps[:, SLOTS + g % T_BANKS, :],
                                        gate[:, 4 * mixer:4 * mixer + 4, :].rearrange("p c q -> p (c q)"),
                                        ALU.mult).then_inc(prod_done, 1)

            def low_part(c):
                dve.wait_ge(y_hi_done, c + 1)
                nc.vector.tensor_tensor(prod[:, c % 2, :].bitcast(F32R), prod[:, c % 2, :], y[:, c % 2, :],
                                        ALU.subtract).then_inc(y_lo_done, 1)

            for s in range(S + LAG + 3):
                if s < S:
                    if s % STEPS == 0:
                        open_block(s // STEPS)
                    scores(s)
                if s - LAG - 3 in closing:
                    low_part(closing[s - LAG - 3])
                if s - LAG - 1 in closing:
                    normalise(closing[s - LAG - 1])
                if s - LAG - 2 in closing:
                    gated(closing[s - LAG - 2])
def project_out(nc, x, w_out, final_g, scr, out):
    MT = scr["y"].shape[3]
    HALF = D_MODEL // 2
    with ExitStack() as ctx:
        def sb(name, shape, dt=F32):
            return ctx.enter_context(nc.sbuf_tensor("o_" + name, shape, dt))

        def sem(name):
            return ctx.enter_context(nc.semaphore("o_" + name))

        ps = ctx.enter_context(nc.psum_tensor("o_ps", [P, 8, 512], F32))
        w_raw = sb("w_raw", [P, 3, D_MODEL])
        w_hi = sb("w_hi", [P, MT, D_MODEL], F32R)
        w_lo = sb("w_lo", [P, MT, D_MODEL], F32R)
        yt = sb("yt", [P, 2, 2, MT, P], F32R)
        xt = sb("xt", [P, 2, D_MODEL])
        res = sb("res", [P, 2, D_MODEL])
        junk = sb("junk", [P, D_MODEL])
        g = sb("g", [P, D_MODEL])
        norm = sb("norm", [P, BLOCKS, 6])

        g_in = sem("g_in")
        w_in_sem, w_hi_done, w_lo_done = [sem(f"w_in{i}") for i in range(3)], sem("w_hi_done"), sem("w_lo_done")
        y_in, x_in = [sem(f"y_in{i}") for i in range(2)], [sem(f"x_in{i}") for i in range(2)]
        mixed, added, sq_done, ms_done = sem("mixed"), sem("added"), sem("sq_done"), sem("ms_done")
        root_done, newton, scaled = sem("root_done"), sem("newton"), sem("scaled")
        out_st = [sem(f"out_st{i}") for i in range(2)]

        block = ctx.enter_context(nc.Block())

        @block.sync
        def _(sp):
            def load_block(b):
                if b >= 2:
                    sp.wait_ge(mixed, b - 1)
                for part in range(2):
                    sp.dma_start(yt[:, b % 2, part].bitcast(F32), scr["y"][part, b]).then_inc(y_in[b % 2], 16)
                if b >= 2:
                    sp.wait_ge(added, b - 1)
                sp.dma_start(xt[:, b % 2, :], x[0, P * b:P * b + P, :]).then_inc(x_in[b % 2], 16)

            def load_w(k):
                if k >= 3:
                    sp.wait_ge(w_hi_done, k - 2)
                    sp.wait_ge(w_lo_done, k - 2)
                sp.dma_start(w_raw[:, k % 3, :], w_out[0, P * k:P * k + P, :]).then_inc(w_in_sem[k % 3], 16)

            load_w(0)
            load_w(1)
            load_block(0)
            for k in range(2, MT):
                load_w(k)
            sp.dma_start(g[:], final_g.partition_broadcast(P)).then_inc(g_in, 16)
            load_block(1)
            for b in range(BLOCKS):
                if b + 2 < BLOCKS:
                    load_block(b + 2)
                sp.wait_ge(scaled, b + 1)
                sp.dma_start(out[0, P * b:P * b + P, :], res[:, b % 2, :]).then_inc(out_st[b % 2], 16)
            for i in range(2):
                sp.wait_ge(out_st[i], 16 * (BLOCKS // 2))

        @block.tensor
        def _(pe):
            for b in range(BLOCKS):
                bank = 2 * (b % 4)
                pe.wait_ge(y_in[b % 2], 32 * (b // 2 + 1))
                if b >= 4:
                    pe.wait_ge(added, b - 3)
                for k in range(MT):
                    if b == 0:
                        pe.wait_ge(w_hi_done, k + 1)
                        pe.wait_ge(w_lo_done, k + 1)
                    for i, (yp, w) in enumerate(((0, w_hi), (0, w_lo), (1, w_hi))):
                        for c in range(2):
                            ins = nc.tensor.matmul(ps[:, bank + c, :], yt[:, b % 2, yp, k, :],
                                                   w[:, k, HALF * c:HALF * c + HALF],
                                                   start=(k == 0 and i == 0), stop=(k == MT - 1 and i == 2))
                ins.then_inc(mixed, 1)

        @block.scalar
        def _(act):
            for k in range(MT):
                act.wait_ge(w_in_sem[k % 3], 16 * (k // 3 + 1))
                nc.scalar.activation(w_hi[:, k, :], w_raw[:, k % 3, :], ACT.Copy).then_inc(w_hi_done, 1)
            for b in range(BLOCKS):
                act.wait_ge(added, b + 1)
                nc.scalar.activation(junk[:], res[:, b % 2, :], ACT.Square,
                                     accum_out=norm[:, b, 0:1]).then_inc(sq_done, 1)
                act.wait_ge(ms_done, b + 1)
                nc.scalar.activation(norm[:, b, 2:3], norm[:, b, 1:2], ACT.Sqrt).then_inc(root_done, 1)

        @block.vector
        def _(dve):
            for k in range(MT):
                dve.wait_ge(w_hi_done, k + 1)
                nc.vector.tensor_tensor(w_lo[:, k, :], w_raw[:, k % 3, :], w_hi[:, k, :].bitcast(F32),
                                        ALU.subtract).then_inc(w_lo_done, 1)
            dve.wait_ge(g_in, 16)
            for b in range(BLOCKS):
                dve.wait_ge(mixed, b + 1)
                dve.wait_ge(x_in[b % 2], 16 * (b // 2 + 1))
                if b >= 2:
                    dve.wait_ge(out_st[b % 2], 16 * (b // 2))
                bank = 2 * (b % 4)
                nc.vector.tensor_tensor(res[:, b % 2, :], ps[:, bank:bank + 2, :].rearrange("p a b -> p (a b)"),
                                        xt[:, b % 2, :], ALU.add).then_inc(added, 1)
                dve.wait_ge(sq_done, b + 1)
                nc.vector.tensor_scalar(norm[:, b, 1:2], norm[:, b, 0:1], 1.0 / D_MODEL, EPS,
                                        ALU.mult, ALU.add).then_inc(ms_done, 1)
                dve.wait_ge(root_done, b + 1)
                mean, y = norm[:, b, 1:2], norm[:, b, 3:4]
                nc.vector.reciprocal(y, norm[:, b, 2:3]).then_inc(newton, 1)
                dve.wait_ge(newton, 4 * b + 1)
                nc.vector.tensor_scalar(norm[:, b, 4:5], y, y, mean, ALU.mult, ALU.mult).then_inc(newton, 1)
                dve.wait_ge(newton, 4 * b + 2)
                nc.vector.tensor_scalar(norm[:, b, 5:6], norm[:, b, 4:5], -0.5, 1.5, ALU.mult, ALU.add).then_inc(newton, 1)
                dve.wait_ge(newton, 4 * b + 3)
                nc.vector.tensor_scalar(y, y, norm[:, b, 5:6], None, ALU.mult).then_inc(newton, 1)
                dve.wait_ge(newton, 4 * b + 4)
                nc.vector.scalar_tensor_tensor(out=res[:, b % 2, :], in0=res[:, b % 2, :], scalar=y, in1=g[:],
                                               op0=ALU.mult, op1=ALU.mult).then_inc(scaled, 1)


def scratch(nc):
    def dram(name, shape, dt=F32):
        return nc.dram_tensor("s_" + name, shape, dt, kind="Internal").ap()

    scr = {n: dram(n, (BLOCKS, 2, DH, HEADS, P)) for n in ("q_a", "q_i", "q_b", "q_c")}
    scr |= {n: dram(n, (2, DH, heads, NKEY)) for n, heads in (("k_a", HEADS), ("k_c", HEADS), ("k_i", 1), ("k_b", KV_B))}
    scr |= {n: dram(n, (NKEY, w)) for n, w in (("v_a", HEADS * DH), ("v_c", HEADS * DH), ("v_b", KV_B * DH))}
    scr["w_i"] = dram("w_i", (P, BLOCKS, HEADS))
    scr["gate"] = dram("gate", (BLOCKS, P, 12, P))
    scr["sel"] = dram("sel", (BLOCKS, P, NKEY), BF16)
    scr["y"] = dram("y", (2, BLOCKS, P, 12, P))
    return scr


def build(nc, t, out):
    scr = scratch(nc)
    with ExitStack() as ctx:
        h_hi = ctx.enter_context(nc.sbuf_tensor("h_hi", [P, KT, NKEY], F32R))
        h_lo = ctx.enter_context(nc.sbuf_tensor("h_lo", [P, KT, NKEY], F32R))
        project(nc, t["x"], t["meta_tokens"], t["norm_g"], t["w_in"], t["kv_norm_g"], t["w_uk"], t["w_uv"],
                t["ident"], h_hi, h_lo, scr)
        project_and_select(nc, t["w_in"], t["q_scale"], t["halves"], h_hi, h_lo, scr)
    stick_breaking(nc, t["ident"], t["stick_mask"], scr)
    softmax_mixers(nc, t["ident"], t["distance"], t["band_distance"], t["neg_slope"], t["sinks"], scr)
    project_out(nc, t["x"], t["w_out"], t["final_norm_g"], scr, out)


def constants():
    f = np.float32
    r, q = np.arange(P)[:, None], np.arange(P)[None]
    slope = 2.0 ** -(np.arange(HEADS) + 1.0)
    distance = -np.abs(r - (np.arange(NKEY)[None] - (NKEY - P)))
    band = np.full((BLOCKS, P, BAND), -BIG)
    near = np.arange(-64, 0)[None]
    for j in range(BLOCKS):
        band[j, :, 0:N_META] = -(N_META + P * j + r - np.arange(N_META)[None])
        if j:
            band[j, :, N_META:NEAR] = np.where(r < 64, -np.abs(r - near), -BIG)
        band[j, :, NEAR:] = np.where((r >= 64) | (q < 64), -np.abs(r - q), -BIG)
    head = 2 * np.arange(4)[None] + (r >= 64)
    return {"ident": np.eye(P, dtype=f), "q_scale": (DH ** -0.5 / slope[head]).astype(f),
            "stick_mask": np.where(q >= r, -BIG, 0.0).astype(f),
            "halves": np.broadcast_to(2.0 ** -(np.arange(ROUNDS) + 1.0), (P, ROUNDS)).astype(f),
            "distance": distance.astype(f), "band_distance": band.astype(f),
            "neg_slope": np.broadcast_to(-slope, (P, HEADS)).astype(f)}


def kernel(x, meta_tokens, norm_g, w_in, kv_norm_g, w_uk, w_uv, sinks, w_out, final_norm_g):
    import concourse.bacc as bacc
    from concourse.bass_utils import run_bass_kernel_spmd

    given = {"x": x, "meta_tokens": meta_tokens, "norm_g": np.asarray(norm_g).reshape(KT, P).T,
             "w_in": w_in, "kv_norm_g": np.asarray(kv_norm_g).reshape(P, 1), "w_uk": w_uk, "w_uv": w_uv,
             "sinks": sinks, "w_out": w_out, "final_norm_g": final_norm_g} | constants()
    given = {k: np.ascontiguousarray(v) for k, v in given.items()}
    nc = bacc.Bacc("TRN2", target_bir_lowering=False, num_devices=1)
    t = {k: nc.dram_tensor("in_" + k, v.shape, mybir.dt.from_np(v.dtype), kind="ExternalInput").ap()
         for k, v in given.items()}
    out = nc.dram_tensor("out", (1, SEQ, D_MODEL), F32, kind="ExternalOutput").ap()
    build(nc, t, out)
    result = run_bass_kernel_spmd(nc, [{"in_" + k: v for k, v in given.items()}], core_ids=[0])
    return result.results[0]["out"]
```
